# Optimizing a Trainium2 kernel written in Bass

```python
import math
import jax, jax.numpy as jnp
from jax import lax
import numpy as np

D_MODEL = 1024
BATCH = 1
SEQ = 512
DEPTH = 1

MEM_LEN = 256

MLA_HEADS = 8
QK_NOPE = 64
QK_ROPE = 32
V_HEAD = 64
Q_LORA = 256
KV_LORA = 256
ROPE_THETA = 10000.0
Q_BLOCK = 128

S5_GROUP_CH = 16
S5_WIDTH = 512
S5_GROUPS = S5_WIDTH // S5_GROUP_CH
S5_STATE = 64
DT_MIN = 1e-3
DT_MAX = 1e-1

XATTN_HEADS = 4
XATTN_HEAD_DIM = 128

N_EXPERTS = 64
TOP_K = 8
N_EXPERT_GROUPS = 8
TOPK_GROUPS = 4
EXPERT_FF = 256
SHARED_FF = 256
ROUTED_SCALE = 2.5
MOE_BLOCK = 128

LN_EPS = 1e-5
RMS_EPS = 1e-6

DEEPNORM_ALPHA = (2.0 * DEPTH) ** 0.25
DEEPNORM_BETA = (8.0 * DEPTH) ** -0.25

IN_SIZES = (Q_LORA, KV_LORA, QK_ROPE, S5_WIDTH, D_MODEL, D_MODEL)
IN_WIDTH = sum(IN_SIZES)
IN_OFFSETS = tuple(int(v) for v in np.cumsum(IN_SIZES)[:-1])


def layer_norm(x, g, b):
    xf = x.astype(jnp.float32)
    mu = jnp.mean(xf, axis=-1, keepdims=True)
    var = jnp.mean(jnp.square(xf - mu), axis=-1, keepdims=True)
    y = (xf - mu) * lax.rsqrt(var + LN_EPS) * g.astype(jnp.float32) + b.astype(jnp.float32)
    return y.astype(x.dtype)

def rms_norm(x, g):
    xf = x.astype(jnp.float32)
    y = xf * lax.rsqrt(jnp.mean(jnp.square(xf), axis=-1, keepdims=True) + RMS_EPS)
    return (y * g.astype(jnp.float32)).astype(x.dtype)

def rope_cos_sin(positions):
    inv_freq = ROPE_THETA ** (-jnp.arange(0, QK_ROPE, 2, dtype=jnp.float32) / QK_ROPE)
    ang = positions.astype(jnp.float32)[..., None] * inv_freq
    return jnp.cos(ang), jnp.sin(ang)

def apply_rope(x, cos, sin):
    cos = cos.astype(x.dtype)
    sin = sin.astype(x.dtype)
    x1, x2 = jnp.split(x, 2, axis=-1)
    return jnp.concatenate([x1 * cos - x2 * sin, x2 * cos + x1 * sin], axis=-1)

def causal_block_attention(q_nope, q_rope, k_nope, k_rope, v):
    B, S, H, _ = q_nope.shape
    nb = S // Q_BLOCK
    scale = (QK_NOPE + QK_ROPE) ** -0.5
    qn_b = q_nope.reshape(B, nb, Q_BLOCK, H, QK_NOPE).transpose(1, 0, 2, 3, 4)
    qr_b = q_rope.reshape(B, nb, Q_BLOCK, H, QK_ROPE).transpose(1, 0, 2, 3, 4)
    key_pos = jnp.arange(S)

    def one_block(args):
        i, qn, qr = args
        s = (jnp.einsum('bqhd,bkhd->bhqk', qn, k_nope)
             + jnp.einsum('bqhr,bkr->bhqk', qr, k_rope)).astype(jnp.float32) * scale
        q_pos = i * Q_BLOCK + jnp.arange(Q_BLOCK)
        mask = key_pos[None, :] <= q_pos[:, None]
        s = jnp.where(mask[None, None], s, -jnp.inf)
        p = jax.nn.softmax(s, axis=-1).astype(v.dtype)
        return jnp.einsum('bhqk,bkhd->bqhd', p, v)

    out = lax.map(one_block, (jnp.arange(nb), qn_b, qr_b))
    return out.transpose(1, 0, 2, 3, 4).reshape(B, S, H, V_HEAD)

def mla_branch(h_q, h_kv, k_rope_raw, positions, q_norm_g, kv_norm_g, w_uq, w_ukv, w_mla_o):
    B, S, _ = h_q.shape
    q = (rms_norm(h_q, q_norm_g) @ w_uq).reshape(B, S, MLA_HEADS, QK_NOPE + QK_ROPE)
    q_nope, q_rope = q[..., :QK_NOPE], q[..., QK_NOPE:]
    kv = (rms_norm(h_kv, kv_norm_g) @ w_ukv).reshape(B, S, MLA_HEADS, QK_NOPE + V_HEAD)
    k_nope, v = kv[..., :QK_NOPE], kv[..., QK_NOPE:]
    cos, sin = rope_cos_sin(positions)
    q_rope = apply_rope(q_rope, cos[:, :, None, :], sin[:, :, None, :])
    k_rope = apply_rope(k_rope_raw, cos, sin)
    attn = causal_block_attention(q_nope, q_rope, k_nope, k_rope, v)
    return attn.reshape(B, S, MLA_HEADS * V_HEAD) @ w_mla_o

def _complex_affine_combine(c1, c2):
    a1r, a1i, b1r, b1i = c1
    a2r, a2i, b2r, b2i = c2
    ar = a2r * a1r - a2i * a1i
    ai = a2r * a1i + a2i * a1r
    br = a2r * b1r - a2i * b1i + b2r
    bi = a2r * b1i + a2i * b1r + b2i
    return (ar, ai, br, bi)

def s5_branch(u, a_re, a_im, log_dt, b_re, b_im, c_re, c_im, d, w_glu):
    B, S, _ = u.shape
    f32 = jnp.float32
    uf = u.astype(f32).reshape(B, S, S5_GROUPS, S5_GROUP_CH)
    dt = jnp.exp(log_dt.astype(f32))[:, None]
    ar, ai = a_re.astype(f32), a_im.astype(f32)
    mag = jnp.exp(ar * dt)
    abar_r, abar_i = mag * jnp.cos(ai * dt), mag * jnp.sin(ai * dt)
    den = ar * ar + ai * ai
    nr, ni = abar_r - 1.0, abar_i
    coef_r = ((nr * ar + ni * ai) / den)[..., None]
    coef_i = ((ni * ar - nr * ai) / den)[..., None]
    br, bi = b_re.astype(f32), b_im.astype(f32)
    bbar_r = coef_r * br - coef_i * bi
    bbar_i = coef_r * bi + coef_i * br
    bu_r = jnp.einsum('bsgh,gph->bsgp', uf, bbar_r)
    bu_i = jnp.einsum('bsgh,gph->bsgp', uf, bbar_i)
    a_r = jnp.broadcast_to(abar_r, bu_r.shape)
    a_i = jnp.broadcast_to(abar_i, bu_i.shape)
    _, _, xr, xi = lax.associative_scan(_complex_affine_combine, (a_r, a_i, bu_r, bu_i), axis=1)
    y = (jnp.einsum('bsgp,ghp->bsgh', xr, c_re.astype(f32))
         - jnp.einsum('bsgp,ghp->bsgh', xi, c_im.astype(f32)))
    y = y.reshape(B, S, S5_WIDTH) + d.astype(f32) * uf.reshape(B, S, S5_WIDTH)
    y = jax.nn.gelu(y).astype(u.dtype)
    val, gate = jnp.split(y @ w_glu, 2, axis=-1)
    return val * jax.nn.sigmoid(gate)

def hybrid_mixer(x, positions, w_in, q_norm_g, kv_norm_g, w_uq, w_ukv, w_mla_o,
                 s5_a_re, s5_a_im, s5_log_dt, s5_b_re, s5_b_im, s5_c_re, s5_c_im,
                 s5_d, w_s5_glu, w_out):
    proj = x @ w_in
    h_q, h_kv, k_rope_raw, u, g_mla, g_s5 = jnp.split(proj, IN_OFFSETS, axis=-1)
    y_mla = mla_branch(h_q, h_kv, k_rope_raw, positions, q_norm_g, kv_norm_g, w_uq, w_ukv, w_mla_o)
    y_s5 = s5_branch(u, s5_a_re, s5_a_im, s5_log_dt, s5_b_re, s5_b_im, s5_c_re, s5_c_im, s5_d, w_s5_glu)
    merged = jax.nn.sigmoid(g_mla) * y_mla + jax.nn.sigmoid(g_s5) * y_s5
    return merged @ w_out

def memory_cross_attention(x, mem, mem_ln_g, mem_ln_b, w_xq, w_xkv, w_xo):
    B, S, _ = x.shape
    M = mem.shape[1]
    m = layer_norm(mem, mem_ln_g, mem_ln_b)
    q = (x @ w_xq).reshape(B, S, XATTN_HEADS, XATTN_HEAD_DIM)
    kv = (m @ w_xkv).reshape(B, M, 2, XATTN_HEADS, XATTN_HEAD_DIM)
    k, v = kv[:, :, 0], kv[:, :, 1]
    s = jnp.einsum('bshd,bmhd->bhsm', q, k).astype(jnp.float32) * (XATTN_HEAD_DIM ** -0.5)
    p = jax.nn.softmax(s, axis=-1).astype(v.dtype)
    o = jnp.einsum('bhsm,bmhd->bshd', p, v).reshape(B, S, XATTN_HEADS * XATTN_HEAD_DIM)
    return o @ w_xo

def swiglu(x, w_gu, w_down):
    g, u = jnp.split(x @ w_gu, 2, axis=-1)
    return (jax.nn.silu(g) * u) @ w_down

def moe_ffn(x2d, w_router, router_bias, w_exp_gu, w_exp_down, w_sh_gu, w_sh_down):
    T, D = x2d.shape
    scores = jax.nn.sigmoid((x2d @ w_router).astype(jnp.float32))
    sel = scores + router_bias.astype(jnp.float32)
    per_group = N_EXPERTS // N_EXPERT_GROUPS
    grp_score = lax.top_k(sel.reshape(T, N_EXPERT_GROUPS, per_group), 2)[0].sum(-1)
    _, grp_idx = lax.top_k(grp_score, TOPK_GROUPS)
    grp_mask = jax.nn.one_hot(grp_idx, N_EXPERT_GROUPS, dtype=jnp.float32).sum(1) > 0
    sel = jnp.where(jnp.repeat(grp_mask, per_group, axis=1), sel, -jnp.inf)
    _, top_idx = lax.top_k(sel, TOP_K)
    w = jnp.take_along_axis(scores, top_idx, axis=1)
    w = w / jnp.sum(w, axis=-1, keepdims=True) * ROUTED_SCALE

    A = T * TOP_K
    flat_e = top_idx.reshape(A).astype(jnp.int32)
    flat_tok = jnp.repeat(jnp.arange(T, dtype=jnp.int32), TOP_K)
    flat_w = w.reshape(A).astype(x2d.dtype)
    order = jnp.argsort(flat_e)
    se = flat_e[order]
    counts = jnp.zeros((N_EXPERTS,), jnp.int32).at[flat_e].add(1)
    starts = jnp.cumsum(counts) - counts
    padded = (counts + MOE_BLOCK - 1) // MOE_BLOCK * MOE_BLOCK
    pends = jnp.cumsum(padded)
    pstarts = pends - padded
    dest = pstarts[se] + (jnp.arange(A, dtype=jnp.int32) - starts[se])
    n_blocks = (A + N_EXPERTS * (MOE_BLOCK - 1) + MOE_BLOCK - 1) // MOE_BLOCK
    P = n_blocks * MOE_BLOCK
    buf_tok = jnp.full((P,), T, jnp.int32).at[dest].set(flat_tok[order])
    buf_w = jnp.zeros((P,), x2d.dtype).at[dest].set(flat_w[order])
    block_start = jnp.arange(n_blocks, dtype=jnp.int32) * MOE_BLOCK
    block_e = jnp.minimum(jnp.searchsorted(pends, block_start, side='right'), N_EXPERTS - 1)
    x_pad = jnp.concatenate([x2d, jnp.zeros((1, D), x2d.dtype)], axis=0)

    def expert_block(args):
        tok, e = args
        return swiglu(x_pad[tok], w_exp_gu[e], w_exp_down[e])

    out = lax.map(expert_block, (buf_tok.reshape(n_blocks, MOE_BLOCK), block_e))
    out = out.reshape(P, D) * buf_w[:, None]
    routed = jnp.zeros((T + 1, D), x2d.dtype).at[buf_tok].add(out)[:T]
    return routed + swiglu(x2d, w_sh_gu, w_sh_down)

def first_inputs(seed: int = 0) -> dict:
    key = jax.random.key(seed)
    ks = iter(jax.random.split(key, 48))
    L, D = DEPTH, D_MODEL
    f32 = jnp.float32

    def nrm(shape, scale):
        return jax.random.normal(next(ks), shape, f32) * scale

    def gain(shape):
        return 1.0 + 0.02 * jax.random.normal(next(ks), shape, f32)

    x = jax.random.normal(next(ks), (BATCH, SEQ, D), f32)
    mem = jax.random.normal(next(ks), (BATCH, MEM_LEN, D), f32)
    positions = (jnp.arange(SEQ, dtype=jnp.int32)[None, :]
                 + jax.random.randint(next(ks), (BATCH, 1), 0, 1024, jnp.int32))
    a_re = -0.5 + 0.01 * jax.random.normal(next(ks), (L, S5_GROUPS, S5_STATE), f32)
    a_im = (jnp.pi * jnp.arange(S5_STATE, dtype=f32))[None, None, :] \
        + 0.01 * jax.random.normal(next(ks), (L, S5_GROUPS, S5_STATE), f32)
    log_dt = jax.random.uniform(next(ks), (L, S5_GROUPS), f32, math.log(DT_MIN), math.log(DT_MAX))
    beta = DEEPNORM_BETA
    return {
        "x": x,
        "mem": mem,
        "positions": positions,
        "w_in": nrm((L, D, IN_WIDTH), D ** -0.5),
        "q_norm_g": gain((L, Q_LORA)),
        "kv_norm_g": gain((L, KV_LORA)),
        "w_uq": nrm((L, Q_LORA, MLA_HEADS * (QK_NOPE + QK_ROPE)), Q_LORA ** -0.5),
        "w_ukv": nrm((L, KV_LORA, MLA_HEADS * (QK_NOPE + V_HEAD)), KV_LORA ** -0.5),
        "w_mla_o": nrm((L, MLA_HEADS * V_HEAD, D), (MLA_HEADS * V_HEAD) ** -0.5),
        "s5_a_re": a_re,
        "s5_a_im": a_im,
        "s5_log_dt": log_dt,
        "s5_b_re": nrm((L, S5_GROUPS, S5_STATE, S5_GROUP_CH), (2 * S5_GROUP_CH) ** -0.5),
        "s5_b_im": nrm((L, S5_GROUPS, S5_STATE, S5_GROUP_CH), (2 * S5_GROUP_CH) ** -0.5),
        "s5_c_re": nrm((L, S5_GROUPS, S5_GROUP_CH, S5_STATE), (2 * S5_STATE) ** -0.5 * 4.0),
        "s5_c_im": nrm((L, S5_GROUPS, S5_GROUP_CH, S5_STATE), (2 * S5_STATE) ** -0.5 * 4.0),
        "s5_d": nrm((L, S5_WIDTH), 1.0),
        "w_s5_glu": nrm((L, S5_WIDTH, 2 * D), S5_WIDTH ** -0.5),
        "w_out": nrm((L, D, D), D ** -0.5 * beta),
        "ln1_g": gain((L, D)),
        "ln1_b": nrm((L, D), 0.02),
        "mem_ln_g": gain((L, D)),
        "mem_ln_b": nrm((L, D), 0.02),
        "w_xq": nrm((L, D, XATTN_HEADS * XATTN_HEAD_DIM), D ** -0.5),
        "w_xkv": nrm((L, D, 2 * XATTN_HEADS * XATTN_HEAD_DIM), D ** -0.5),
        "w_xo": nrm((L, XATTN_HEADS * XATTN_HEAD_DIM, D), (XATTN_HEADS * XATTN_HEAD_DIM) ** -0.5 * beta),
        "ln2_g": gain((L, D)),
        "ln2_b": nrm((L, D), 0.02),
        "w_router": nrm((L, D, N_EXPERTS), D ** -0.5),
        "router_bias": nrm((L, N_EXPERTS), 0.01),
        "w_exp_gu": nrm((L, N_EXPERTS, D, 2 * EXPERT_FF), D ** -0.5),
        "w_exp_down": nrm((L, N_EXPERTS, EXPERT_FF, D), EXPERT_FF ** -0.5 * beta),
        "w_sh_gu": nrm((L, D, 2 * SHARED_FF), D ** -0.5),
        "w_sh_down": nrm((L, SHARED_FF, D), SHARED_FF ** -0.5 * beta),
        "ln3_g": gain((L, D)),
        "ln3_b": nrm((L, D), 0.02),
    }

def first_block(x, mem, positions, w_in, q_norm_g, kv_norm_g, w_uq, w_ukv, w_mla_o,
              s5_a_re, s5_a_im, s5_log_dt, s5_b_re, s5_b_im, s5_c_re, s5_c_im, s5_d,
              w_s5_glu, w_out, ln1_g, ln1_b, mem_ln_g, mem_ln_b, w_xq, w_xkv, w_xo,
              ln2_g, ln2_b, w_router, router_bias, w_exp_gu, w_exp_down, w_sh_gu,
              w_sh_down, ln3_g, ln3_b):
    B, S, D = x.shape
    for l in range(DEPTH):
        mix = hybrid_mixer(x, positions, w_in[l], q_norm_g[l], kv_norm_g[l], w_uq[l], w_ukv[l],
                           w_mla_o[l], s5_a_re[l], s5_a_im[l], s5_log_dt[l], s5_b_re[l],
                           s5_b_im[l], s5_c_re[l], s5_c_im[l], s5_d[l], w_s5_glu[l], w_out[l])
        x = layer_norm(DEEPNORM_ALPHA * x + mix, ln1_g[l], ln1_b[l])
        xa = memory_cross_attention(x, mem, mem_ln_g[l], mem_ln_b[l], w_xq[l], w_xkv[l], w_xo[l])
        x = layer_norm(DEEPNORM_ALPHA * x + xa, ln2_g[l], ln2_b[l])
        ff = moe_ffn(x.reshape(B * S, D), w_router[l], router_bias[l], w_exp_gu[l],
                     w_exp_down[l], w_sh_gu[l], w_sh_down[l]).reshape(B, S, D)
        x = layer_norm(DEEPNORM_ALPHA * x + ff, ln3_g[l], ln3_b[l])
    return x


_first_inputs = first_inputs


def first_inputs(seed=0):
    import zlib

    import numpy as np

    out = dict(_first_inputs(seed))
    spreads = {}
    factors = {'q_norm_g': 8.0,
     'kv_norm_g': 8.0,
     's5_a_re': 8.0,
     'mem_ln_g': 7.491,
     'ln3_g': 2.851,
     'ln3_b': 2.942}
    for name, (base, spread) in spreads.items():
        noise = np.random.default_rng([zlib.crc32(name.encode()), seed]).standard_normal(out[name].shape)
        drawn = base * np.exp(spread * noise) if base else spread * noise
        out[name] = __import__('jax').numpy.asarray(drawn.astype(out[name].dtype))
    for name, factor in factors.items():
        out[name] = (out[name] * factor).astype(out[name].dtype)
    return out


_narrow_inputs = first_inputs


def first_inputs(seed=0):
    out = dict(_narrow_inputs(seed))
    wider = {'s5_a_re': 12.0, 'mem_ln_b': 4.76, 'ln3_g': 3.21, 'ln3_b': 3.21}
    for name, times in wider.items():
        mean = out[name].mean()
        out[name] = (mean + times * (out[name] - mean)).astype(out[name].dtype)
    return out


D_MIX = D_MODEL
D_A = D_MIX // 2
D_B = D_MIX - D_A
HEAD_DIM = 64
H_A = D_A // HEAD_DIM
H_B = D_B // HEAD_DIM
N_KV = 2
GQA = H_B // N_KV
D_KV = N_KV * HEAD_DIM
CHUNK = 128
CMP_BLOCK = 32
CMP_STRIDE = 16
CMP_HIDDEN = 256
SEL_BLOCK = 64
N_SELECT = 16
WINDOW = 512
N_GATES = 3
D_IN = 2 * D_A + D_B + 6 * D_KV + N_GATES * H_B
D_FF = int(math.ceil(8 * D_MODEL / 3 / 256)) * 256
EPS = 1e-6
NEG = -1e30
FORCE = 1e4


def rmsnorm(x, w):
    xf = x.astype(jnp.float32)
    y = xf * lax.rsqrt(jnp.mean(xf * xf, axis=-1, keepdims=True) + EPS)
    return (y * w.astype(jnp.float32)).astype(x.dtype)

def masked_softmax(s, mask):
    p = jax.nn.softmax(jnp.where(mask, s.astype(jnp.float32), NEG), axis=-1)
    return jnp.where(mask, p, 0.0)

def split_offsets():
    sizes = [D_A, D_A, D_B, D_KV, D_KV, D_KV, D_KV, D_KV, D_KV, N_GATES * H_B]
    return [int(o) for o in np.cumsum(sizes)[:-1]]

def gmlp_group(u, v, norm_w, ws, bs):
    B, S, _ = u.shape
    nc = S // CHUNK
    u = jax.nn.gelu(u).reshape(B, nc, CHUNK, H_A, HEAD_DIM)
    v = rmsnorm(jax.nn.gelu(v), norm_w).reshape(B, nc, CHUNK, H_A, HEAD_DIM)
    causal = jnp.tril(jnp.ones((CHUNK, CHUNK), dtype=bool))
    w = jnp.where(causal[None], ws, 0).astype(v.dtype)
    sv = jnp.einsum('hts,bcshd->bcthd', w, v) + bs.T.astype(v.dtype)[None, None, :, :, None]
    return (u * sv).reshape(B, S, D_A)

def compress(kv, pos, w1, w2):
    B, S = kv.shape[0], kv.shape[1]
    n_cmp = (S - CMP_BLOCK) // CMP_STRIDE + 1
    idx = jnp.arange(n_cmp)[:, None] * CMP_STRIDE + jnp.arange(CMP_BLOCK)[None, :]
    blk = kv[:, idx] + pos[None, None, :, None, :]
    blk = blk.transpose(0, 1, 3, 2, 4).reshape(B, n_cmp, N_KV, CMP_BLOCK * HEAD_DIM)
    return jax.nn.gelu(blk @ w1) @ w2

def nsa_group(q, k_c, v_c, k_s, v_s, k_w, v_w, g_raw,
              cmp_pos_k, cmp_pos_v, cmp_k_w1, cmp_k_w2, cmp_v_w1, cmp_v_w2, gate_b):
    B, S = q.shape[0], q.shape[1]
    q = (q * (HEAD_DIM ** -0.5)).reshape(B, S, N_KV, GQA, HEAD_DIM)
    kv_shape = (B, S, N_KV, HEAD_DIM)
    k_c, v_c, k_s, v_s, k_w, v_w = [a.reshape(kv_shape) for a in (k_c, v_c, k_s, v_s, k_w, v_w)]
    t = jnp.arange(S)
    n_qb = S // Q_BLOCK

    kc = compress(k_c, cmp_pos_k, cmp_k_w1, cmp_k_w2)
    vc = compress(v_c, cmp_pos_v, cmp_v_w1, cmp_v_w2)
    n_cmp = kc.shape[1]
    cmp_start = jnp.arange(n_cmp) * CMP_STRIDE
    cmp_mask = (cmp_start + CMP_BLOCK - 1)[None, :] <= t[:, None]
    s_cmp = jnp.einsum('bskgd,bnkd->bkgsn', q, kc)
    p_cmp = masked_softmax(s_cmp, cmp_mask)
    o_cmp = jnp.einsum('bkgsn,bnkd->bskgd', p_cmp.astype(vc.dtype), vc)

    n_blk = S // SEL_BLOCK
    n_sel = min(N_SELECT, n_blk)
    blk_start = jnp.arange(n_blk) * SEL_BLOCK
    overlap = ((cmp_start[:, None] < blk_start[None, :] + SEL_BLOCK)
               & (cmp_start[:, None] + CMP_BLOCK > blk_start[None, :])).astype(jnp.float32)
    imp = jnp.einsum('bkgsn,nj->bksj', p_cmp, overlap)
    cur = t // SEL_BLOCK
    j = jnp.arange(n_blk)
    valid = j[None, :] <= cur[:, None]
    forced = (j[None, :] == 0) | (j[None, :] == cur[:, None]) | (j[None, :] == cur[:, None] - 1)
    score = jnp.where(forced, FORCE, jnp.where(valid, imp, -FORCE))
    _, sel = lax.top_k(score, n_sel)
    sel = sel.transpose(0, 2, 1, 3)

    kb = k_s.reshape(B, n_blk, SEL_BLOCK, N_KV, HEAD_DIM).transpose(0, 3, 1, 2, 4)
    vb = v_s.reshape(B, n_blk, SEL_BLOCK, N_KV, HEAD_DIM).transpose(0, 3, 1, 2, 4)
    b_ix = jnp.arange(B)[:, None, None, None]
    h_ix = jnp.arange(N_KV)[None, None, :, None]

    def sel_block(args):
        qc, ic, tc = args
        kg = kb[b_ix, h_ix, ic]
        vg = vb[b_ix, h_ix, ic]
        pos = ic[..., None] * SEL_BLOCK + jnp.arange(SEL_BLOCK)
        mask = (pos <= tc[None, :, None, None, None]).reshape(B, Q_BLOCK, N_KV, 1, n_sel * SEL_BLOCK)
        s = jnp.einsum('bqkgd,bqknrd->bqkgnr', qc, kg).reshape(B, Q_BLOCK, N_KV, GQA, n_sel * SEL_BLOCK)
        p = masked_softmax(s, mask)
        vg = vg.reshape(B, Q_BLOCK, N_KV, n_sel * SEL_BLOCK, HEAD_DIM)
        return jnp.einsum('bqkgm,bqkmd->bqkgd', p.astype(vg.dtype), vg)

    qs = q.reshape(B, n_qb, Q_BLOCK, N_KV, GQA, HEAD_DIM).transpose(1, 0, 2, 3, 4, 5)
    sels = sel.reshape(B, n_qb, Q_BLOCK, N_KV, n_sel).transpose(1, 0, 2, 3, 4)
    ts = t.reshape(n_qb, Q_BLOCK)
    o_slc = lax.map(sel_block, (qs, sels, ts))
    o_slc = o_slc.transpose(1, 0, 2, 3, 4, 5).reshape(B, S, N_KV, GQA, HEAD_DIM)

    span = WINDOW + Q_BLOCK
    pad = ((0, 0), (WINDOW, 0), (0, 0), (0, 0))
    band = jnp.arange(n_qb)[:, None] * Q_BLOCK + jnp.arange(span)[None, :]
    kw = jnp.pad(k_w, pad)[:, band]
    vw = jnp.pad(v_w, pad)[:, band]
    kpos = band - WINDOW
    diff = ts[:, :, None] - kpos[:, None, :]
    win_mask = (diff >= 0) & (diff < WINDOW) & (kpos[:, None, :] >= 0)
    qw = q.reshape(B, n_qb, Q_BLOCK, N_KV, GQA, HEAD_DIM)
    s_win = jnp.einsum('bcqkgd,bcmkd->bckgqm', qw, kw)
    p_win = masked_softmax(s_win, win_mask[None, :, None, None])
    o_win = jnp.einsum('bckgqm,bcmkd->bcqkgd', p_win.astype(vw.dtype), vw).reshape(B, S, N_KV, GQA, HEAD_DIM)

    g = jax.nn.sigmoid(g_raw + gate_b).reshape(B, S, N_GATES, N_KV, GQA, 1)
    o = g[:, :, 0] * o_cmp + g[:, :, 1] * o_slc + g[:, :, 2] * o_win
    return o.reshape(B, S, D_B)

def second_inputs(seed: int = 0) -> dict:
    key = jax.random.key(seed)
    ks = iter(jax.random.split(key, 32))

    def nrm(shape, scale):
        return jax.random.normal(next(ks), shape, jnp.float32) * scale

    def gain(shape):
        return 1.0 + nrm(shape, 0.01)

    L = DEPTH
    return {
        "x": nrm((BATCH, SEQ, D_MODEL), 1.0),
        "norm_mix_w": gain((L, D_MODEL)),
        "w_in": nrm((L, D_MODEL, D_IN), D_MODEL ** -0.5),
        "gmlp_norm_w": gain((L, D_A)),
        "gmlp_ws": nrm((L, H_A, CHUNK, CHUNK), 0.5 * CHUNK ** -0.5),
        "gmlp_bs": 1.0 + nrm((L, H_A, CHUNK), 0.01),
        "cmp_pos_k": nrm((L, CMP_BLOCK, HEAD_DIM), 0.1),
        "cmp_pos_v": nrm((L, CMP_BLOCK, HEAD_DIM), 0.1),
        "cmp_k_w1": nrm((L, CMP_BLOCK * HEAD_DIM, CMP_HIDDEN), (CMP_BLOCK * HEAD_DIM) ** -0.5),
        "cmp_k_w2": nrm((L, CMP_HIDDEN, HEAD_DIM), CMP_HIDDEN ** -0.5),
        "cmp_v_w1": nrm((L, CMP_BLOCK * HEAD_DIM, CMP_HIDDEN), (CMP_BLOCK * HEAD_DIM) ** -0.5),
        "cmp_v_w2": nrm((L, CMP_HIDDEN, HEAD_DIM), CMP_HIDDEN ** -0.5),
        "gate_b": nrm((L, N_GATES * H_B), 0.01),
        "out_norm_a_w": gain((L, D_A)),
        "out_norm_b_w": gain((L, D_B)),
        "w_o": nrm((L, D_MIX, D_MODEL), D_MIX ** -0.5),
        "norm_ffn_w": gain((L, D_MODEL)),
        "w_gate": nrm((L, D_MODEL, D_FF), D_MODEL ** -0.5),
        "w_up": nrm((L, D_MODEL, D_FF), D_MODEL ** -0.5),
        "w_down": nrm((L, D_FF, D_MODEL), D_FF ** -0.5),
        "final_norm_w": gain((D_MODEL,)),
    }

def second_block(x, norm_mix_w, w_in, gmlp_norm_w, gmlp_ws, gmlp_bs,
              cmp_pos_k, cmp_pos_v, cmp_k_w1, cmp_k_w2, cmp_v_w1, cmp_v_w2,
              gate_b, out_norm_a_w, out_norm_b_w, w_o, norm_ffn_w,
              w_gate, w_up, w_down, final_norm_w):
    offsets = split_offsets()
    for l in range(DEPTH):
        h = rmsnorm(x, norm_mix_w[l])
        z = h @ w_in[l]
        u, v, q, k_c, v_c, k_s, v_s, k_w, v_w, g_raw = jnp.split(z, offsets, axis=-1)
        a = gmlp_group(u, v, gmlp_norm_w[l], gmlp_ws[l], gmlp_bs[l])
        b = nsa_group(q, k_c, v_c, k_s, v_s, k_w, v_w, g_raw,
                      cmp_pos_k[l], cmp_pos_v[l], cmp_k_w1[l], cmp_k_w2[l],
                      cmp_v_w1[l], cmp_v_w2[l], gate_b[l])
        mix = jnp.concatenate([rmsnorm(a, out_norm_a_w[l]), rmsnorm(b, out_norm_b_w[l])], axis=-1)
        x = x + mix @ w_o[l]
        h = rmsnorm(x, norm_ffn_w[l])
        x = x + (jax.nn.silu(h @ w_gate[l]) * (h @ w_up[l])) @ w_down[l]
    return rmsnorm(x, final_norm_w)


_first_inputs_2 = second_inputs


def second_inputs(seed=0):
    import zlib

    import numpy as np

    out = dict(_first_inputs_2(seed))
    spreads = {}
    factors = {'norm_mix_w': 6.381,
     'gmlp_norm_w': 64.0,
     'gmlp_bs': 48.476,
     'cmp_pos_k': 5.802,
     'gate_b': 49.652,
     'out_norm_a_w': 46.307,
     'out_norm_b_w': 48.521,
     'norm_ffn_w': 33.148,
     'final_norm_w': 34.207,
     'cmp_pos_v': 7.836}
    for name, (base, spread) in spreads.items():
        noise = np.random.default_rng([zlib.crc32(name.encode()), seed]).standard_normal(out[name].shape)
        drawn = base * np.exp(spread * noise) if base else spread * noise
        out[name] = __import__('jax').numpy.asarray(drawn.astype(out[name].dtype))
    for name, factor in factors.items():
        out[name] = (out[name] * factor).astype(out[name].dtype)
    return out


_narrow_inputs_2 = second_inputs


def second_inputs(seed=0):

    out = dict(_narrow_inputs_2(seed))
    wider = {'gmlp_norm_w': 12.0,
     'gmlp_bs': 7.16,
     'out_norm_a_w': 6.61,
     'out_norm_b_w': 6.62,
     'norm_ffn_w': 4.61,
     'final_norm_w': 6.64}
    for name, times in wider.items():
        mean = out[name].mean()
        out[name] = (mean + times * (out[name] - mean)).astype(out[name].dtype)
    return out


def setup_inputs(seed=0):
    out = dict(first_inputs(seed))
    for name, value in second_inputs(seed + 1).items():
        if name != "x":
            out[name + "_2"] = value
    return out


def reference(
    x, mem, positions, w_in, q_norm_g, kv_norm_g, w_uq, w_ukv, w_mla_o, s5_a_re, s5_a_im,
    s5_log_dt, s5_b_re, s5_b_im, s5_c_re, s5_c_im, s5_d, w_s5_glu, w_out, ln1_g, ln1_b,
    mem_ln_g, mem_ln_b, w_xq, w_xkv, w_xo, ln2_g, ln2_b, w_router, router_bias, w_exp_gu,
    w_exp_down, w_sh_gu, w_sh_down, ln3_g, ln3_b, norm_mix_w_2, w_in_2, gmlp_norm_w_2,
    gmlp_ws_2, gmlp_bs_2, cmp_pos_k_2, cmp_pos_v_2, cmp_k_w1_2, cmp_k_w2_2, cmp_v_w1_2,
    cmp_v_w2_2, gate_b_2, out_norm_a_w_2, out_norm_b_w_2, w_o_2, norm_ffn_w_2, w_gate_2, w_up_2,
    w_down_2, final_norm_w_2,
):
    x = first_block(
        x, mem, positions, w_in, q_norm_g, kv_norm_g, w_uq, w_ukv, w_mla_o, s5_a_re, s5_a_im,
        s5_log_dt, s5_b_re, s5_b_im, s5_c_re, s5_c_im, s5_d, w_s5_glu, w_out, ln1_g, ln1_b,
        mem_ln_g, mem_ln_b, w_xq, w_xkv, w_xo, ln2_g, ln2_b, w_router, router_bias, w_exp_gu,
        w_exp_down, w_sh_gu, w_sh_down, ln3_g, ln3_b,
    )
    return second_block(
        x, norm_mix_w_2, w_in_2, gmlp_norm_w_2, gmlp_ws_2, gmlp_bs_2, cmp_pos_k_2, cmp_pos_v_2,
        cmp_k_w1_2, cmp_k_w2_2, cmp_v_w1_2, cmp_v_w2_2, gate_b_2, out_norm_a_w_2,
        out_norm_b_w_2, w_o_2, norm_ffn_w_2, w_gate_2, w_up_2, w_down_2, final_norm_w_2,
    )


_drawn_inputs = setup_inputs


def setup_inputs(seed=0):
    import zlib

    import numpy as np

    out = dict(_drawn_inputs(seed))
    spreads = {}
    factors = {}
    for name, (base, spread) in spreads.items():
        noise = np.random.default_rng([zlib.crc32(name.encode()), seed]).standard_normal(out[name].shape)
        drawn = base * np.exp(spread * noise) if base else spread * noise
        out[name] = __import__('jax').numpy.asarray(drawn.astype(out[name].dtype))
    for name, factor in factors.items():
        out[name] = (out[name] * factor).astype(out[name].dtype)
    return out
```

```python
from contextlib import ExitStack

import numpy as np

import concourse.bass as bass
from concourse import mybir

F32 = mybir.dt.float32
I32 = mybir.dt.int32
U32 = mybir.dt.uint32
ALU = mybir.AluOpType
ACT = mybir.ActivationFunctionType
AX = mybir.AxisListType.X

P = 128
T = 512
NT = T // P
D = 1024
KD = D // P
NMEM = 256
H1, NOPE, ROPE = 8, 64, 32
XH, XD = 4, 128
NG, NS, NCH = 32, 64, 16
NST = NG * NS // P
NE, TOPK, NGRP, TOPG = 64, 8, 8, 4
NOV = 31
NBLK = NE + NOV
TABW = 96
FF = 256
NV2 = 16
NC_ = 31
FT = 22
ALPHA = 2.0 ** 0.25
RSCALE = 2.5
BIG = 1.0e30
MAGIC = 12582912.0
MAGIC12 = 3072.0
TWO_PI_HI = 6.28125
TWO_PI_LO = 0.0019353071795864769
SIN_SCALE = 6.283185
PI_LIM = 3.1415925
RING = 12
PW_ = 1024

COLS = {}


def _cols():
    at = 0
    for name, n in (("q_norm_g", 2), ("kv_norm_g", 2), ("mem_g", 8), ("mem_b", 8), ("s5_d", 4),
                    ("norm_mix", 8), ("out_a", 4), ("out_b", 4), ("norm_ffn", 8), ("a_re", 16),
                    ("a_im", 16), ("log_dt", 16), ("gmlp_bs", 8), ("pos_k", 16), ("pos_v", 16),
                    ("freq", 2), ("phase", 2), ("sign", 2)):
        COLS[name] = (at, n)
        at += n
    COLS["width"] = at


_cols()
ROWS = ["ln1_g", "ln1_b", "ln2_g", "ln2_b", "ln3_g", "ln3_b", "final", "gmlp_norm", "gate_b", "router_bias"]


NORM = {"hq": 0, "mem": 4, "ln1": 6, "ln2": 10, "h2": 14, "h4": 18, "final": 22}


def _requests():
    r, n = [(8, 8)], 0
    for k in (2, 4, 4, 4, 4):
        for _ in range(k):
            r.append((n % 8, 1))
            n += 1
    r += [(8, 4), (12, 4), (8, 4)]
    for k in (4, 4):
        for _ in range(k):
            r.append((n % 8, 1))
            n += 1
    return r


REQUESTS = _requests()


class Plan:

    def __init__(self, order, banks):
        self.n, self.read, self.by, self.where, self.before = {}, {}, {}, {}, {}
        count = {"act": 0, "dve": 0}
        last = {}
        at = 0
        for k, (name, i, by) in enumerate(order):
            key = (name, i)
            assert key not in self.n, key
            self.n[key] = k + 1
            count[by] += 1
            self.read[key] = count[by]
            self.by[key] = by
            bank = banks - 1 if name == "s5y" else at % (banks - 1)
            at += name != "s5y"
            self.where[key] = bank
            self.before[key] = last.get(bank)
            last[bank] = key
        self.total = len(order)

    def full(self, name, i):
        return self.n[name, i]

    def done(self, name, i):
        return self.read[name, i]


def psum_order():
    o = []
    add = lambda name, i, by: o.append((name, i, by))

    def s5_in(i):
        add("s5r", i, "dve")
        add("s5i", i, "dve")

    def s5_out(i):
        if i % 4 == 3:
            add("s5y", i // 4, "dve")

    for i in range(4):
        add("u", i, "act")
    for t in range(NT):
        add("hqkv", t, "act")
        s5_in(t)
    add("krope", 0, "dve")
    for c in range(4):
        add("hT", c, "act")
    for h in range(H1):
        add("q", h, "dve")
        if h in (1, 3, 5):
            s5_in(4 + h // 2)
            s5_out(h // 2)
    for c in range(4):
        add("kn", c, "act")
    for t in range(NT):
        add("v", t, "act")
    for h in range(H1 + 2):
        if h < H1:
            for qt in range(NT):
                add("s", 4 * h + qt, "act")
        if h >= 2:
            add("o", h - 2, "act")
        if h < H1:
            s5_in(7 + h)
        elif h == H1:
            s5_in(15)
        s5_out(3 + h)
        if 1 <= h <= H1:
            for qt in range(NT):
                add("pt", 4 * (h - 1) + qt, "act" if qt % 2 else "dve")
    for m in range(KD):
        add("gm", m, "act")
        add("ym", m, "dve")
        if m < 3:
            s5_out(13 + m)
    for m in range(KD):
        add("gs", m, "act")
        add("gate", m, "act")
        add("val", m, "dve")
        if m >= 4:
            add("memT", m - 4, "act")
    for i in range(8):
        add("mix", i, "dve")
    for h in range(XH):
        add("kx", h, "act")
    for t in range(2):
        add("vx", t, "act")
    for c in range(KD):
        add("x1T", c, "act" if c % 2 else "dve")
    for h in range(XH):
        add("xq", h, "act")
    for h in range(XH + 2):
        if h < XH:
            for qt in range(NT):
                add("xs", 4 * h + qt, "act")
        if h >= 2:
            add("xo", h - 2, "act")
        if 1 <= h <= XH:
            for qt in range(NT):
                add("xpt", 4 * (h - 1) + qt, "act" if qt % 2 else "dve")
    for i in range(8):
        add("xa", i, "dve")
    for c in range(KD):
        add("x2T", c, "act" if c % 2 else "dve")
    for t in range(NT):
        add("lg", t, "act")
    for c in range(2):
        add("sg", c, "act")
        add("su", c, "dve")
    for i in range(8):
        add("sd", i, "dve")
    add("pos", 0, "dve")
    for c in range(KD):
        add("hT2", c, "act")
    for i in range(8):
        add("uv", i, "act")
    for c in range(4):
        add("zq", c, "act")
    for c in range(2):
        add("kc", c, "dve")
    for c in range(2):
        add("ksw", c, "act")
    for t in range(NT):
        add("vs", t, "act")
    for h in range(8):
        add("sv", h, "dve")
    for c in range(4):
        add("ck", c, "act")
    add("kcc", 0, "act")
    add("vcc", 0, "act")
    for qt in range(NT):
        add("sc", qt, "dve")
    for c in range(4):
        add("aT", c, "act")
    for i in range(8):
        add("woa", i, "dve")
    for qt in range(NT):
        add("pct", qt, "dve")
    for v in range(NV2 + 2):
        if v < NV2:
            for qt in range(NT):
                add("s2", 4 * v + qt, "act")
        if 1 <= v <= NV2:
            for qt in range(NT):
                add("pt2", 4 * (v - 1) + qt, "act" if qt % 2 else "dve")
        if v >= 3 and v % 2 == 1:
            add("o2", (v - 3) // 2, "act")
    add("sb", 0, "dve")
    for i in range(8):
        add("wob", i, "dve")
    for c in range(KD):
        add("h4T", c, "act" if c % 2 else "dve")
    for f in range(FT):
        add("fg", f, "act")
        add("fu", f, "dve")
    for i in range(8):
        add("fd", i, "dve")
    return o


def panel_plan():
    p = [("u", i, ("u", i)) for i in range(4)]
    p += [("hqkv", i, ("hqkv", 3)) for i in range(4)]
    p += [("krope", 0, ("krope", 0))]
    p += [("q", i, ("q", 4 * i + 3)) for i in range(2)]
    p += [("kn", 0, ("kn", 3)), ("v", 0, ("v", 3))]
    for m in range(KD):
        p += [("gm", m, ("gm", m))]
        if m % 2 == 0:
            p += [("ym", m // 2, ("ym", m + 1))]
    for m in range(KD):
        p += [("gs", m, ("gs", m)), ("glu", m, ("val", m))]
    p += [("mix", k, ("mix", 7)) for k in range(8)]
    p += [("kx", h, ("kx", h)) for h in range(4)]
    p += [("vx", k, ("vx", 1)) for k in range(4)]
    p += [("xq", h, ("xq", h)) for h in range(4)]
    p += [("xa", k, ("xa", 7)) for k in range(4)]
    for c in range(2):
        p += [("sg", c, ("sg", c)), ("su", c, ("su", c))]
    p += [("sd", k, ("sd", 7)) for k in range(2)]
    n1 = len(p)
    p += [("uv", k, ("uv", 7)) for k in range(8)]
    p += [("zq", c, ("zq", c)) for c in range(4)]
    p += [("kc", c, ("kc", c)) for c in range(2)]
    p += [("ksw", c, ("ksw", c)) for c in range(2)]
    p += [("vs", k, ("vs", 3)) for k in range(4)]
    p += [("w1k", k, ("ck", 1)) for k in range(4)]
    p += [("w1v", k, ("ck", 3)) for k in range(4)]
    p += [("woa", k, ("woa", 7)) for k in range(4)]
    p += [("wob", k, ("wob", 7)) for k in range(4)]
    for f in range(FT):
        p += [("fg", f, ("fg", f)), ("fu", f, ("fu", f))]
    p += [("fd", k, ("fd", 4 * (k // 11) + 3) if k % 11 == 10 else ("ffn", k - k // 11)) for k in range(FT)]
    return p, n1


PANELS, N1 = panel_plan()


def host_stream(w):
    f = np.float32

    def a_panel(m, c0, k0=0):
        k = m.shape[0] // P
        return m[:, c0:c0 + P].reshape(k, P, P).transpose(1, 0, 2).reshape(P, k * P)

    def rows(m, k, c0, n):
        return m[k * P:(k + 1) * P, c0:c0 + n]

    def two(m, i, c0, n=512):
        out = np.zeros((P, 2, 512), f)
        for b in range(2):
            out[:, b, :n] = rows(m, 2 * i + b, c0, n)
        return out.reshape(P, 1024)

    w_in, w_uq, w_ukv = w["w_in"][0], w["w_uq"][0], w["w_ukv"][0]
    w2, glu = w["w_in_2"][0], w["w_s5_glu"][0]
    gmla0, gs50 = 1056, 2080
    half = ROPE // 2
    kr = w_in[:, 512:544]
    ks = np.concatenate([kr[:, half:], kr[:, :half]], 1)
    krope = np.concatenate([kr, kr, ks, ks], 1)
    qh = []
    for h in range(H1):
        c = w_uq[:, 96 * h:96 * h + 96]
        qh.append(np.concatenate([c, c[:, 80:96], c[:, 64:80]], 1))
    qh = np.concatenate(qh, 1)
    ukv = w_ukv.reshape(256, H1, 128)
    kn = ukv[:, :, :64].reshape(256, 512)
    vv = ukv[:, :, 64:].reshape(256, 512)
    gu = w["w_sh_gu"][0]
    q2 = w2[:, 1024:1536].reshape(D, 8, 64)
    q2 = np.stack([q2[:, :4], q2[:, 4:]], 2).reshape(D, 512)
    off = 1536
    c2 = {n: w2[:, off + 128 * j:off + 128 * (j + 1)] for j, n in enumerate(("kc", "vc", "ks", "vs", "kw", "vw"))}
    vs = np.concatenate([c2["vs"], c2["vw"], w2[:, 2304:2328]], 1)
    out = np.empty((len(PANELS), P, PW_), f)

    def w1_panel(m, k):
        m = m.reshape(2, 16, 64, 256)[:, 4 * k:4 * k + 4]
        return m.transpose(0, 2, 1, 3).reshape(P, 1024)

    def pair(m, i, n):
        return np.concatenate([a_panel(m, (n * i + j) * P) for j in range(n)], 1)

    make = {
        "u": lambda i: a_panel(w_in, 544 + i * P), "hqkv": lambda i: two(w_in, i, 0),
        "krope": lambda i: a_panel(krope, 0), "q": lambda i: pair(qh, i, 4), "kn": lambda i: pair(kn, i, 4),
        "v": lambda i: two(vv, 0, 0), "gm": lambda i: a_panel(w_in, gmla0 + i * P),
        "ym": lambda i: pair(w["w_mla_o"][0], i, 2), "gs": lambda i: a_panel(w_in, gs50 + i * P),
        "glu": lambda i: np.concatenate([a_panel(glu, D + i * P), a_panel(glu, i * P)], 1),
        "mix": lambda i: rows(w["w_out"][0], i, 0, D), "kx": lambda i: a_panel(w["w_xkv"][0], i * P),
        "vx": lambda i: two(w["w_xkv"][0], i, 512), "xq": lambda i: a_panel(w["w_xq"][0], i * P),
        "xa": lambda i: rows(w["w_xo"][0], i, 0, D), "sg": lambda i: a_panel(gu, i * P),
        "su": lambda i: a_panel(gu, FF + i * P), "sd": lambda i: rows(w["w_sh_down"][0], i, 0, D),
        "uv": lambda i: rows(w2, i, 0, D), "zq": lambda i: a_panel(q2, i * P),
        "kc": lambda i: a_panel(c2[("kc", "vc")[i]], 0), "ksw": lambda i: a_panel(c2[("ks", "kw")[i]], 0),
        "vs": lambda i: two(vs, i, 0, 280), "w1k": lambda i: w1_panel(w["cmp_k_w1_2"][0], i),
        "w1v": lambda i: w1_panel(w["cmp_v_w1_2"][0], i), "woa": lambda i: rows(w["w_o_2"][0], i, 0, D),
        "wob": lambda i: rows(w["w_o_2"][0], 4 + i, 0, D), "fg": lambda i: a_panel(w["w_gate_2"][0], i * P),
        "fu": lambda i: a_panel(w["w_up_2"][0], i * P),
        "fd": lambda i: two(w["w_down_2"][0], i % 11, 512 * (i // 11)),
    }
    for n, (what, i, _) in enumerate(PANELS):
        out[n] = make[what](i)
    return out


def host_consts():
    f = np.float32
    i = np.arange(P)
    c = {}
    c["ident"] = np.eye(P, dtype=f)
    c["causal"] = np.where(i[None, :] > i[:, None], f(-BIG), f(0))
    c["tri"] = (i[:, None] < i[None, :]).astype(f)
    c["keep_ts"] = (i[:, None] <= i[None, :]).astype(f)
    t = np.arange(T).reshape(NT, P).T
    m = (np.arange(NC_)[None, None, :] * 16 + 31) <= t[:, :, None]
    m01 = np.zeros((P, NT, 32), f)
    m01[:, :, :NC_] = m
    c["cmp01"] = m01.reshape(P, NT * 32)
    c["iota64"] = np.tile(np.arange(64, dtype=f), (P, 1))
    g = np.arange(8)
    c["gtri"] = np.tile((g[None, :] < g[:, None]).astype(f).reshape(1, 64), (P, 1))
    c["tokid"] = t.astype(f)
    return c


CONST_AT = {}


def _const_layout():
    at = 0
    for k, v in host_consts().items():
        CONST_AT[k] = (at, v.shape[1])
        at += v.shape[1]
    CONST_AT["width"] = at


_const_layout()


def host_cols(w):
    f = np.float32
    out = np.zeros((P, COLS["width"]), f)

    def put(name, a):
        at, n = COLS[name]
        out[:, at:at + n] = a

    feat = lambda v: v.reshape(-1, P).T
    put("q_norm_g", feat(w["q_norm_g"][0]))
    put("kv_norm_g", feat(w["kv_norm_g"][0]))
    put("mem_g", feat(w["mem_ln_g"][0]))
    put("mem_b", feat(w["mem_ln_b"][0]))
    put("s5_d", feat(w["s5_d"][0]))
    put("norm_mix", feat(w["norm_mix_w_2"][0]))
    put("out_a", feat(w["out_norm_a_w_2"][0]))
    put("out_b", feat(w["out_norm_b_w_2"][0]))
    put("norm_ffn", feat(w["norm_ffn_w_2"][0]))
    put("a_re", feat(w["s5_a_re"][0].reshape(-1)))
    put("a_im", feat(w["s5_a_im"][0].reshape(-1)))
    put("log_dt", feat(np.repeat(w["s5_log_dt"][0], NS)))
    put("gmlp_bs", w["gmlp_bs_2"][0].T)
    for n, a in (("pos_k", w["cmp_pos_k_2"][0]), ("pos_v", w["cmp_pos_v_2"][0])):
        put(n, a.reshape(2, 16, 64).transpose(0, 2, 1).reshape(P, 16))
    inv = (f(10000.0) ** (-np.arange(0, ROPE, 2, dtype=f) / f(ROPE))).astype(f)
    fr = np.concatenate([inv, inv])
    sg = np.concatenate([-np.ones(16, f), np.ones(16, f)])
    freq, phase, sign = np.zeros((P, 2), f), np.zeros((P, 2), f), np.ones((P, 2), f)
    freq[64:, 0] = np.tile(fr, 2)
    phase[64:96, 0] = 1
    sign[96:, 0] = sg
    freq[:, 1] = np.tile(fr, 4)
    phase[:64, 1] = 1
    sign[64:, 1] = np.tile(sg, 2)
    put("freq", freq)
    put("phase", phase)
    put("sign", sign)
    return out


def host_s5(w):
    f = np.float32
    bm = np.zeros((2, P, 4, P), f)
    cm = np.zeros((2, P, NST, 32), f)
    for n, (b, c) in enumerate((("s5_b_re", "s5_c_re"), ("s5_b_im", "s5_c_im"))):
        for i in range(NST):
            for g in range(2):
                grp = 2 * i + g
                r = 32 * (i % 4) + 16 * g
                bm[n, r:r + 16, i // 4, 64 * g:64 * g + 64] = w[b][0, grp].T
                cm[n, 64 * g:64 * g + 64, i, 16 * g:16 * g + 16] = w[c][0, grp].T
    return np.concatenate([bm[0].reshape(P, 512), bm[1].reshape(P, 512),
                           cm[0].reshape(P, 512), cm[1].reshape(P, 512)], 1)


def build(nc, a, out, scratch):
    plan = Plan(psum_order(), 8)
    with ExitStack() as ctx:
        def sb(name, n, dt=F32):
            return ctx.enter_context(nc.sbuf_tensor(name, [P, n], dt))

        def sem(name):
            return ctx.enter_context(nc.semaphore(name))

        bank = [ctx.enter_context(nc.psum_tensor(f"bank{i}", [P, 512], F32)) for i in range(8)]

        def tile(name, i):
            return bank[plan.where[name, i]]

        slab1, slab2, slab3, slab4 = [sb(f"slab{i}", 4096) for i in range(1, 5)]
        slab6, slab7, slab8, slab9 = [sb(f"slab{i}", 2048) for i in range(6, 10)]
        work = sb("work", 6656)
        s5x = sb("s5x", 5120)
        gb = sb("gb", 2048)
        ring = sb("ring", RING * PW_)
        const = sb("const_sb", CONST_AT["width"])
        cols = sb("cols_sb", COLS["width"])
        rope_q = sb("rope_q", T)
        iota_t = sb("iota_t", T)
        small = sb("small", 256)

        def cst(name):
            at, n = CONST_AT[name]
            return const[:, at:at + n]

        def col(name, i):
            at, _ = COLS[name]
            return cols[:, at + i:at + i + 1]

        def colr(name):
            at, n = COLS[name]
            return cols[:, at:at + n]

        def fm(slab, k, at=0):
            return slab[:, at + k * T:at + (k + 1) * T]

        def tm(slab, t):
            return slab[:, t * D:(t + 1) * D]

        ident = cst("ident")
        sm_at = [0]

        def sm(n):
            at = sm_at[0]
            sm_at[0] += n
            assert sm_at[0] <= 256
            return small[:, at:at + n]

        xT = slab1
        qhat, khat = slab2, slab3
        hq = work[:, 0:2048].rearrange("p (t n) -> p t n", t=4)
        hT = work[:, 2048:4096]
        v_tok = slab6[:, :].rearrange("p (t n) -> p t n", t=4)
        oT = slab7
        rope_k, krope, krope_t = slab7[:, 0:512], slab7[:, 512:1024], slab7[:, 1024:1536]
        s5tmp = slab7[:, 1536:2048]
        uT = slab8
        yT = slab9
        unit = lambda j: (slab4[:, j * T:(j + 1) * T] if j < 8 else s5x[:, (j - 8) * T:(j - 7) * T])
        s5u, s5k, s5f = unit(0), unit(1), unit(2)
        s5cos, s5sin = [unit(3), unit(4)], [unit(5), unit(6)]
        s5wr, s5wi = unit(7), unit(8)
        s5zr, s5zi = [unit(9), unit(10)], [unit(11), unit(12)]
        s5xr, s5xi, s5xt = [unit(13), unit(14)], [unit(15), unit(16)], unit(17)
        b_re = gb[:, 0:512].rearrange("p (j n) -> p j n", j=4)
        b_im = gb[:, 512:1024].rearrange("p (j n) -> p j n", j=4)
        c_re = gb[:, 1024:1536].rearrange("p (i n) -> p i n", i=NST)
        c_im = gb[:, 1536:2048].rearrange("p (i n) -> p i n", i=NST)
        phi, phi_hi, phi_lo, mag = sm(16), sm(16), sm(16), sm(16)
        pofs = [0, 128, 384, 768]

        def probs(v, qt, w=None):
            w = (qt + 1) * P if w is None else w
            at = (v % 2) * 1280 + pofs[qt]
            return work[:, at:at + w]

        def probsT(v):
            at = 2560 + (v % 2) * 2048
            return work[:, at:at + 2048].rearrange("p (k n) -> p k n", k=4)

        merged = slab2
        sig_a, sig_b = [fm(work, 0), fm(work, 1)], [fm(work, 2), fm(work, 3)]
        gated = [fm(work, 4), fm(work, 5)]
        xtok, x1 = slab3, slab4
        memtok = [work[:, 3072:4096], work[:, 4096:5120]]
        memT = slab6
        kxT = slab8[:, 0:1024].rearrange("p (h n) -> p h n", h=4)
        vx = slab8[:, 1024:2048].rearrange("p (t n) -> p t n", t=2)
        x1T, xqT, oxT, x2, x2T = slab1, slab7, slab9, slab3, slab2
        w_rt = s5x[:, 0:512].rearrange("p (k n) -> p k n", k=KD)
        cmpw2 = s5x[:, 512:768].rearrange("p (j c n) -> p j c n", j=2, c=2)
        actT = s5x[:, 1024:2048]
        gate_b, rt_bias, cneg = s5x[:, 768:792], s5x[:, 3300:3364], s5x[:, 3600:3728]
        shsig = [s5x[:, 2048:2560], s5x[:, 2560:3072]]
        acc = slab4

        def xprobs(h, qt):
            at = (h % 2) * 1280 + qt * 256
            return work[:, at:at + 256]

        rt_at = [0]

        def rt(n):
            at = rt_at[0]
            rt_at[0] += n
            assert rt_at[0] <= 6656
            return work[:, at:at + n]

        score, sel, selm, sel_rep, chosen = [rt(256) for _ in range(5)]
        top2, gscore = rt(256), rt(32)
        cmp_a, cmp_b = rt(64), rt(64)
        grank, gkeep, gpen = rt(32), rt(32), rt(32)
        topv, topi, topf = rt(32), rt(32), rt(32)
        pos_sb, q_blk, r_in, blk, addr, yrow = [rt(256) for _ in range(6)]
        t256, t256b = rt(256), rt(256)
        cnt, ovn, ovincl, ovbase = rt(64), rt(64), rt(64), rt(64)
        onehot, oneprod = rt(512), rt(512)
        wsum, wk = rt(4), sm(32)
        addr_k, yrow_k = rt(32), rt(32)
        blk_cmp, blk_exp = slab1[:, 0:2048], rt(32)
        ones_f = ctx.enter_context(nc.sbuf_tensor("ones_f", [P, P], F32))
        addr_i = ctx.enter_context(nc.sbuf_tensor("addr_i", [P, 32], I32))
        yrow_i = ctx.enter_context(nc.sbuf_tensor("yrow_i", [P, 32], I32))
        tok_i = ctx.enter_context(nc.sbuf_tensor("tok_i", [P, 4], I32))
        ctrl_i = ctx.enter_context(nc.sbuf_tensor("ctrl_i", [1, 32], I32))
        slot_tok = s5x[:, 3072:3072 + TABW].bitcast(I32)
        zero_i = s5x[:, 3200:3200 + TABW].bitcast(I32)
        xg = [slab6[:, 0:1024], slab6[:, 1024:2048]]
        xe = [slab7[:, 0:1024].rearrange("p (k n) -> p k n", k=8), slab7[:, 1024:2048].rearrange("p (k n) -> p k n", k=8)]
        ye = [slab8[:, 0:1024], slab8[:, 1024:2048]]
        gsilu = [slab9[:, 0:256], slab9[:, 256:512]]
        hid = [slab9[:, 512:768], slab9[:, 768:1024]]
        hidT = [slab9[:, 1024:1280].rearrange("p (k n) -> p k n", k=2), slab9[:, 1280:1536].rearrange("p (k n) -> p k n", k=2)]
        idx_cur = slab9[:, 1536:1538].bitcast(I32)
        ygath = [slab1[:, j * D:(j + 1) * D] for j in range(4)]

        x3, hid2, h2T = slab3, slab4, slab2
        ug = slab1[:, 0:2048].rearrange("p (t n) -> p t n", t=4)
        vg = slab1[:, 2048:4096].rearrange("p (t n) -> p t n", t=4)
        wsT = work[:, 0:1024].rearrange("p (h n) -> p h n", h=8)
        q2T = slab6
        kcA = slab7[:, 0:1024].rearrange("p (j n) -> p j n", j=2)
        vcA = slab7[:, 1024:2048].rearrange("p (j n) -> p j n", j=2)
        ksT, kwT = slab8[:, 0:512], slab8[:, 512:1024]
        vsw = slab8[:, 1024:2048].rearrange("p (t n) -> p t n", t=4)
        gates = s5x[:, 800:896].rearrange("p (t n) -> p t n", t=4)
        aT = slab9
        h1k, h1v = s5x[:, 1024:1152].rearrange("p (c n) -> p c n", c=2), s5x[:, 1152:1280].rearrange("p (c n) -> p c n", c=2)
        cbias = s5x[:, 896:900]
        kcT, vcR = s5x[:, 1280:1344].rearrange("p (j n) -> p j n", j=2), s5x[:, 1344:1472].rearrange("p (j n) -> p j n", j=2)
        scs = s5x[:, 1536:1536 + 1024].rearrange("p (t h n) -> p t h n", t=4, h=8)
        pcT = s5x[:, 2560:2560 + 1024].rearrange("p (j n) -> p j n", j=2)
        smax_c, ssum_c, fac_c = s5x[:, 900:932], s5x[:, 932:964], s5x[:, 964:996]
        bT = slab7
        bsq = slab1[:, 2048:4096]
        x4, h4, h4T = slab4, slab3, slab1
        actf = ([fm(slab2, k) for k in range(8)] + [fm(slab3, k) for k in range(8)]
                + [fm(slab6, k) for k in range(4)] + [fm(slab7, k) for k in range(2)])
        fsilu = [fm(slab8, 0), fm(slab8, 1)]
        outb = slab1

        nmax, rsum, rinv, fac = sm(4), sm(4), sm(4), sm(4)
        var, rstd = sm(16), sm(16)
        minus_half = sm(8)
        stats = sm(2 * 12)
        mv = sm(2 * 8)
        sumsq = sm(8)
        rstd_a, rstd_b, rstd_v = sm(4), sm(4), sm(4)
        half_pi = sm(1)
        shift = sm(4)
        spare = sm(1)
        tiny = sm(8)

        psum_full = sem("psum_full")
        act_evac = sem("act_evac")
        dve_evac = sem("dve_evac")
        landed = [sem(f"landed{i}") for i in range(RING)]
        in_x, in_const, in_rows = sem("in_x"), sem("in_const"), sem("in_rows")
        in_s5, in_pos, in_xtok, in_mem, in_ln, in_misc = [sem(f"in_{n}") for n in ("s5", "pos", "xtok", "mem", "ln", "misc")]
        act_step, dve_step, pool_step = sem("act_step"), sem("dve_step"), sem("pool_step")
        var_ready, rstd_ready = sem("var_ready"), sem("rstd_ready")
        sumsq_ready = sem("sumsq_ready")
        norm_ready = sem("norm_ready")
        pool_init, s5_phi, s5_uk_sem, s5_frac = sem("pool_init"), sem("s5_phi"), sem("s5_uk"), sem("s5_frac")
        s5_tab, s5_z, s5_x, s5_used, s5_c = sem("s5_tab"), sem("s5_z"), sem("s5_x"), sem("s5_used"), sem("s5_c")
        rope_arg, rope_tab, krope_ready, khat_ready = sem("rope_arg"), sem("rope_tab"), sem("krope_ready"), sem("khat_ready")
        max_ready, probs_ready = sem("max_ready"), sem("probs_ready")
        y_ready, gelu_ready = sem("y_ready"), sem("gelu_ready")
        merged_ready = sem("merged_ready")
        x2_stored, tab_zero = sem("x2_stored"), sem("tab_zero")
        route_mask, route_addr, route_ctrl = sem("route_mask"), sem("route_addr"), sem("route_ctrl")
        ids_sent, ids_back, idx_ready = sem("ids_sent"), sem("ids_back"), sem("idx_ready")
        gathered = [sem("gathered0"), sem("gathered1")]
        gu_landed, dn_landed = [sem("gu_landed0"), sem("gu_landed1")], [sem("dn_landed0"), sem("dn_landed1")]
        y_stored = [sem("y_stored0"), sem("y_stored1")]
        xtr_full, xe_ready, gu_full, silu_ready = sem("xtr_full"), sem("xe_ready"), sem("gu_full"), sem("silu_ready")
        hid_ready, htr_full, hidT_ready, dn_full = sem("hid_ready"), sem("htr_full"), sem("hidT_ready"), sem("dn_full")
        ye_act, ye_dve = sem("ye_act"), sem("ye_dve")
        ov = {n: sem("ov_" + n) for n in ("gather", "w", "store", "xtr", "xe", "gu", "silu", "hid", "htr", "hidT", "dn",
                                          "yact", "ydve", "idx")}
        ygot = [sem(f"ygot{j}") for j in range(4)]
        combined, y_zeroed = sem("combined"), sem("y_zeroed")
        act_ready = sem("act_ready")
        ws_masked, vhat_ready = sem("ws_masked"), sem("vhat_ready")
        cmp_ready, cmp_exp = sem("cmp_ready"), sem("cmp_exp")
        ffn_used = sem("ffn_panel_used")
        out_stored = sem("out_stored")

        def slot(n):
            return (n if n < N1 else n - N1) % RING

        def uses(n):
            if n < N1:
                return n // RING + 1
            before = len([m for m in range(N1) if m % RING == slot(n)])
            return before + (n - N1) // RING + 1

        panel_at = {(w, i): n for n, (w, i, _) in enumerate(PANELS)}

        def panel(what, i):
            n = panel_at[what, i]
            return ring[:, slot(n) * PW_:(slot(n) + 1) * PW_]

        block = ctx.enter_context(nc.Block())

        @block.sync
        def _(sp):
            sp.dma_start(xT[:, :], a["x_fm"]).then_inc(in_x, 16)

            def load_panel(n):
                if n >= RING:
                    if n < N1:
                        key = PANELS[n - RING][2]
                        sp.wait_ge(psum_full, plan.full(*key))
                    elif n - N1 >= RING:
                        key = PANELS[n - RING][2]
                        if key[0] == "ffn":
                            sp.wait_ge(ffn_used, key[1] + 1)
                        else:
                            sp.wait_ge(psum_full, plan.full(*key))
                sp.dma_start(ring[:, slot(n) * PW_:(slot(n) + 1) * PW_], a["stream"][n]).then_inc(landed[slot(n)], 16)

            for n in range(4):
                load_panel(n)
            sp.dma_start(cols[:, :], a["cols"]).then_inc(in_const, 16)
            sp.dma_start(const[:, :], a["const"]).then_inc(in_const, 16)
            sp.dma_start(gb[:, :], a["s5"]).then_inc(in_s5, 16)
            for n in range(4, N1):
                load_panel(n)

            def expert_weights(u, b):
                e = 2 * u + b
                sp.dma_start(ring[:, 6 * b * PW_:(6 * b + 4) * PW_].rearrange("p (k n) -> p k n", k=8),
                             a["w_exp_gu"][e].rearrange("(k p) n -> p k n", p=P)).then_inc(gu_landed[b], 16)
                sp.dma_start(ring[:, (6 * b + 4) * PW_:(6 * b + 6) * PW_].rearrange("p (k n) -> p k n", k=2),
                             a["w_exp_down"][e].rearrange("(k p) n -> p k n", p=P)).then_inc(dn_landed[b], 16)

            for b in range(2):
                held = [PANELS[n][2] for n in range(N1 - RING, N1) if 6 * b <= slot(n) < 6 * b + 6]
                sp.wait_ge(psum_full, max(plan.full(*k) for k in held))
                expert_weights(0, b)
            with sp.Fori(1, NE // 2) as u:
                for b in range(2):
                    sp.wait_ge(dn_full, 2 * u + b - 1)
                    expert_weights(u, b)

            sp.wait_ge(route_ctrl, 2)
            sp.wait_ge(dn_full, NE)
            n_ov = sp.value_load(ctrl_i[0:1, 31:32], min_val=0, max_val=NOV)
            with sp.If(n_ov > 0):
                sp.dma_start(scratch["y"][NE * P:, :], a["zeros"].broadcast_to([NOV * P, D])).then_inc(y_zeroed, 16)
                sp.wait_ge(y_zeroed, 16)
            with sp.Fori(0, NOV) as o:
                with sp.If(n_ov > o):
                    e = sp.value_load(ctrl_i[0:1, bass.ds(o, 1)], min_val=0, max_val=NE - 1)
                    sp.dma_start(ring[:, 0:4 * PW_].rearrange("p (k n) -> p k n", k=8),
                                 a["w_exp_gu"][bass.ds(e, 1)].rearrange("a (k p) n -> p (a k) n", p=P)).then_inc(ov["w"], 16)
                    sp.dma_start(ring[:, 4 * PW_:6 * PW_].rearrange("p (k n) -> p k n", k=2),
                                 a["w_exp_down"][bass.ds(e, 1)].rearrange("a (k p) n -> p (a k) n", p=P)).then_inc(ov["w"], 16)
                    sp.wait_ge(ov["yact"], o + 1)
                    sp.wait_ge(ov["ydve"], o + 1)
                    sp.dma_start(scratch["y"][bass.ds((o + NE) * P, P), :], ye[0]).then_inc(ov["store"], 16)

            for n in range(N1, len(PANELS)):
                load_panel(n)
            for t in range(NT):
                sp.wait_ge(norm_ready, NORM["final"] + t + 1)
                sp.dma_start(out[t * P:(t + 1) * P, :], tm(outb, t)).then_inc(out_stored, 16)
            sp.wait_ge(out_stored, 16 * NT)
            for b in range(2):
                sp.wait_ge(y_stored[b], 16 * NE // 2)

        @block.tensor
        def _(pe):
            closed = [0]

            def free(name, i):
                key = plan.before[name, i]
                if key:
                    pe.wait_ge(act_evac if plan.by[key] == "act" else dve_evac, plan.done(*key))

            def close(mm, name, i):
                closed[0] += 1
                assert plan.full(name, i) == closed[0], (name, i, closed)
                mm.then_inc(psum_full, 1)

            def evac(name, i):
                pe.wait_ge(act_evac if plan.by[name, i] == "act" else dve_evac, plan.done(name, i))

            def need(what, i):
                n = panel_at[what, i]
                pe.wait_ge(landed[slot(n)], 16 * uses(n))

            def product(name, i, lhs, rhs, dst=None, new=True, last=True):
                if new:
                    free(name, i)
                dst = tile(name, i)[:, :] if dst is None else dst
                for k in range(len(lhs)):
                    mm = nc.tensor.matmul(dst, lhs[k], rhs[k], start=(k == 0), stop=(k == len(lhs) - 1))
                if last:
                    close(mm, name, i)
                return mm

            def turn(name, i, blocks, parts=P):
                free(name, i)
                for j, x in enumerate(blocks):
                    mm = nc.tensor.transpose(tile(name, i)[0:parts, j * P:(j + 1) * P], x, ident)
                close(mm, name, i)

            def mcols(what, i, kn, at=0):
                p = panel(what, i)
                return [p[:, (at + k) * P:(at + k + 1) * P] for k in range(kn)]

            def s5_in(i):
                r = slice(32 * (i % 4), 32 * (i % 4) + 32)
                for name, m in (("s5r", b_re), ("s5i", b_im)):
                    product(name, i, [m[r, i // 4, :]], [fm(uT, i // 4)[r, :]])

            def s5_out(i):
                if i % 4 == 0:
                    free("s5y", i // 4)
                pe.wait_ge(s5_x, i + 1)
                r = slice(32 * (i % 4), 32 * (i % 4) + 32)
                dst = tile("s5y", i // 4)[r, :]
                nc.tensor.matmul(dst, c_re[:, i, :], s5xr[i % 2], start=True, stop=False)
                mm = nc.tensor.matmul(dst, c_im[:, i, :], s5xi[i % 2], start=False, stop=True)
                if i % 4 == 3:
                    close(mm, "s5y", i // 4)
                else:
                    mm.then_inc(s5_used, 1)

            def values2(g):
                j, i = g // 4, g % 4
                for w in (2 * g, 2 * g + 1):
                    evac("pt2", 4 * w + 2)
                    evac("pt2", 4 * w + 3)
                if g == 0:
                    evac("vs", 3)
                    evac("vcc", 0)
                    evac("pct", 3)
                free("o2", g)
                r = slice(64 * (g % 2), 64 * (g % 2) + 64)
                q = slice(32 * i, 32 * i + 32)
                nc.tensor.matmul(tile("o2", g)[r, :], vcR[q, j, :], pcT[q, j, :], start=True, stop=False)
                for br in range(2):
                    for k in range(NT):
                        at = 128 * br + 64 * j
                        mm = nc.tensor.matmul(tile("o2", g)[r, k * P:T], vsw[:, k, at:at + 64],
                                              probsT(br)[:, k, k * P:T], start=False, stop=(br == 1 and k == NT - 1))
                close(mm, "o2", g)

            pe.wait_ge(in_x, 16)
            for i in range(4):
                need("u", i)
                product("u", i, mcols("u", i, KD), [fm(xT, k) for k in range(KD)])
            for t in range(NT):
                if t == 0:
                    for k in range(4):
                        need("hqkv", k)
                product("hqkv", t, [fm(xT, k)[:, t * P:(t + 1) * P] for k in range(KD)],
                        [panel("hqkv", k // 2)[:, (k % 2) * 512:(k % 2) * 512 + 512] for k in range(KD)])
                if t == 0:
                    pe.wait_ge(in_s5, 16)
                    pe.wait_ge(in_const, 32)
                    evac("u", 3)
                s5_in(t)
            need("krope", 0)
            product("krope", 0, mcols("krope", 0, KD), [fm(xT, k) for k in range(KD)])
            for c in range(4):
                pe.wait_ge(norm_ready, NORM["hq"] + 4)
                turn("hT", c, [hq[:, t, c * P:(c + 1) * P] for t in range(NT)])
            for h in range(H1):
                if h == 0:
                    evac("hT", 1)
                if h % 4 == 0:
                    need("q", h // 4)
                product("q", h, mcols("q", h // 4, 2, 2 * (h % 4)), [fm(hT, k) for k in range(2)])
                if h in (1, 3, 5):
                    s5_in(4 + h // 2)
                    s5_out(h // 2)
            need("kn", 0)
            evac("hT", 3)
            for c in range(4):
                product("kn", c, mcols("kn", 0, 2, 2 * c), [fm(hT, 2 + k) for k in range(2)])
            need("v", 0)
            for t in range(NT):
                product("v", t, [fm(hT, 2 + k)[:, t * P:(t + 1) * P] for k in range(2)],
                        [panel("v", 0)[:, k * 512:(k + 1) * 512] for k in range(2)])

            for h in range(H1 + 2):
                if h < H1:
                    evac("q", h)
                    evac("kn", h // 2)
                    pe.wait_ge(khat_ready, h + 1)
                    for qt in range(NT):
                        product("s", 4 * h + qt, [fm(qhat, h)[:, qt * P:(qt + 1) * P]],
                                [fm(khat, h)[:, 0:(qt + 1) * P]], tile("s", 4 * h + qt)[:, 0:(qt + 1) * P])
                if h >= 2:
                    g = h - 2
                    evac("pt", 4 * g + 2)
                    evac("pt", 4 * g + 3)
                    evac("v", 3)
                    free("o", g)
                    r = slice(64 * (g % 2), 64 * (g % 2) + 64)
                    for k in range(NT):
                        mm = nc.tensor.matmul(tile("o", g)[r, k * P:T], v_tok[:, k, 64 * g:64 * g + 64],
                                              probsT(g)[:, k, k * P:T], start=(k == 0), stop=(k == NT - 1))
                    close(mm, "o", g)
                if h <= H1:
                    s5_in(7 + h)
                s5_out(3 + h)
                if 1 <= h <= H1:
                    g = h - 1
                    for qt in range(NT):
                        pe.wait_ge(probs_ready, 4 * g + qt + 1)
                        turn("pt", 4 * g + qt, [probs(g, qt)[:, k * P:(k + 1) * P] for k in range(qt + 1)])

            for m in range(KD):
                need("gm", m)
                product("gm", m, mcols("gm", m, KD), [fm(xT, k) for k in range(KD)])
                if m % 2 == 0:
                    need("ym", m // 2)
                if m == 0:
                    evac("o", 7)
                product("ym", m, mcols("ym", m // 2, 4, 4 * (m % 2)), [fm(oT, k) for k in range(4)])
                if m < 3:
                    s5_out(13 + m)
            for m in range(KD):
                need("gs", m)
                product("gs", m, mcols("gs", m, KD), [fm(xT, k) for k in range(KD)])
                need("glu", m)
                if m == 0:
                    pe.wait_ge(gelu_ready, 4)
                product("gate", m, mcols("glu", m, 4), [fm(yT, k) for k in range(4)])
                product("val", m, mcols("glu", m, 4, 4), [fm(yT, k) for k in range(4)])
                if m >= 4:
                    c = m - 4
                    pe.wait_ge(norm_ready, NORM["mem"] + 2)
                    turn("memT", c, [memtok[t][:, (2 * c + j) * P:(2 * c + j + 1) * P] for j in range(2) for t in range(2)])
            pe.wait_ge(merged_ready, 2 * KD)
            for i in range(8):
                t, half = i // 2, i % 2
                if i == 0:
                    for k in range(KD):
                        need("mix", k)
                product("mix", i, [fm(merged, k)[:, t * P:(t + 1) * P] for k in range(KD)],
                        [panel("mix", k)[:, half * 512:half * 512 + 512] for k in range(KD)])
            for h in range(XH):
                need("kx", h)
                if h == 0:
                    evac("memT", 3)
                product("kx", h, mcols("kx", h, KD), [memT[:, k * 256:(k + 1) * 256] for k in range(KD)],
                        tile("kx", h)[:, 0:256])
            for t in range(2):
                if t == 0:
                    for k in range(4):
                        need("vx", k)
                product("vx", t, [memT[:, k * 256 + t * P:k * 256 + (t + 1) * P] for k in range(KD)],
                        [panel("vx", k // 2)[:, (k % 2) * 512:(k % 2) * 512 + 512] for k in range(KD)])
            for c in range(KD):
                pe.wait_ge(norm_ready, NORM["ln1"] + 4)
                turn("x1T", c, [tm(x1, t)[:, c * P:(c + 1) * P] for t in range(NT)])
            for h in range(XH):
                need("xq", h)
                if h == 0:
                    evac("x1T", 6)
                    evac("x1T", 7)
                product("xq", h, mcols("xq", h, KD), [fm(x1T, k) for k in range(KD)])
            for h in range(XH + 2):
                if h < XH:
                    evac("xq", h)
                    evac("kx", h)
                    for qt in range(NT):
                        product("xs", 4 * h + qt, [fm(xqT, h)[:, qt * P:(qt + 1) * P]], [kxT[:, h, :]],
                                tile("xs", 4 * h + qt)[:, 0:256])
                if h >= 2:
                    g = h - 2
                    evac("xpt", 4 * g + 2)
                    evac("xpt", 4 * g + 3)
                    evac("vx", 1)
                    product("xo", g, [vx[:, k, g * P:(g + 1) * P] for k in range(2)],
                            [probsT(g)[:, k, :] for k in range(2)])
                if 1 <= h <= XH:
                    g = h - 1
                    for qt in range(NT):
                        pe.wait_ge(probs_ready, 32 + 4 * g + qt + 1)
                        turn("xpt", 4 * g + qt, [xprobs(g, qt)[:, k * P:(k + 1) * P] for k in range(2)])
            evac("xo", 3)
            for i in range(8):
                t, half = i // 2, i % 2
                if i == 0:
                    for k in range(4):
                        need("xa", k)
                product("xa", i, [fm(oxT, k)[:, t * P:(t + 1) * P] for k in range(4)],
                        [panel("xa", k)[:, half * 512:half * 512 + 512] for k in range(4)])
            for c in range(KD):
                pe.wait_ge(norm_ready, NORM["ln2"] + 4)
                turn("x2T", c, [tm(x2, t)[:, c * P:(c + 1) * P] for t in range(NT)])
            evac("x2T", 6)
            evac("x2T", 7)
            pe.wait_ge(in_misc, 64)
            for t in range(NT):
                product("lg", t, [fm(x2T, k)[:, t * P:(t + 1) * P] for k in range(KD)],
                        [w_rt[:, k, :] for k in range(KD)], tile("lg", t)[:, 0:64])
            for c in range(2):
                for name in ("sg", "su"):
                    need(name, c)
                    product(name, c, mcols(name, c, KD), [fm(x2T, k) for k in range(KD)])
            evac("su", 1)
            for i in range(8):
                t, half = i // 2, i % 2
                if i == 0:
                    need("sd", 0)
                    need("sd", 1)
                product("sd", i, [actT[:, k * T + t * P:k * T + (t + 1) * P] for k in range(2)],
                        [panel("sd", k)[:, half * 512:half * 512 + 512] for k in range(2)])
            pe.wait_ge(route_mask, 1)
            free("pos", 0)
            for t in range(NT):
                for s in range(t + 1):
                    nc.tensor.matmul(tile("pos", 0)[:, 64 * t:64 * t + 64], cst("tri") if s == t else ones_f[:, :],
                                     chosen[:, 64 * s:64 * s + 64], start=(s == 0), stop=(s == t))
            for s in range(NT):
                mm = nc.tensor.matmul(tile("pos", 0)[:, 256:320], ones_f[:, :], chosen[:, 64 * s:64 * s + 64],
                                      start=(s == 0), stop=(s == 3))
            close(mm, "pos", 0)

            for key in [k for k in (("sd", 7), ("pos", 0), ("sd", 6))]:
                evac(*key)

            def turn_rows(b, wait, n, s_free, n_free, s_full):
                pe.wait_ge(wait, n)
                if n_free is not None:
                    pe.wait_ge(s_free, n_free)
                for j in range(2):
                    for k in range(4):
                        mm = nc.tensor.transpose(bank[j][:, k * P:(k + 1) * P], xg[b][:, (4 * j + k) * P:(4 * j + k + 1) * P], ident)
                mm.then_inc(s_full, 1)

            def gate_up(b, s_x, n_x, s_w, n_w, s_full):
                pe.wait_ge(s_x, n_x)
                pe.wait_ge(s_w, n_w)
                for k in range(8):
                    mm = nc.tensor.matmul(bank[2 + b][:, :], xe[b][:, k, :], ring[:, 6 * b * PW_ + k * 512:6 * b * PW_ + (k + 1) * 512],
                                          start=(k == 0), stop=(k == 7))
                mm.then_inc(s_full, 1)

            def turn_hidden(b, s_h, n_h, s_full):
                pe.wait_ge(s_h, n_h)
                for k in range(2):
                    mm = nc.tensor.transpose(bank[4][:, k * P:(k + 1) * P], hid[b][:, k * P:(k + 1) * P], ident)
                mm.then_inc(s_full, 1)

            def down(b, s_h, n_h, s_w, n_w, fre, s_full):
                pe.wait_ge(s_h, n_h)
                pe.wait_ge(s_w, n_w)
                for s, n in fre:
                    pe.wait_ge(s, n)
                at = (6 * b + 4) * PW_
                for half in range(2):
                    for k in range(2):
                        mm = nc.tensor.matmul(bank[5 + half][:, :], hidT[b][:, k, :],
                                              ring[:, at + k * D + half * 512:at + k * D + half * 512 + 512],
                                              start=(k == 0), stop=(k == 1))
                mm.then_inc(s_full, 1)

            def e_turn(u, b, first=False):
                turn_rows(b, gathered[b], 16 * u + 16, xe_ready, None if first else 2 * u + b, xtr_full)

            def e_gu(u, b):
                gate_up(b, xe_ready, 2 * u + b + 1, gu_landed[b], 16 * u + 16, gu_full)

            def e_th(u, b):
                turn_hidden(b, hid_ready, 2 * u + b + 1, htr_full)

            def e_down(u, b, first=False):
                e = 2 * u + b
                down(b, hidT_ready, e + 1, dn_landed[b], 16 * u + 16, [] if first else [(ye_act, e), (ye_dve, e)], dn_full)

            e_turn(0, 0, True)
            e_gu(0, 0)
            e_turn(0, 1)
            e_th(0, 0)
            e_gu(0, 1)
            e_down(0, 0, True)
            e_turn(1, 0)
            e_th(0, 1)
            with pe.Fori(1, NE // 2 - 1) as u:
                e_gu(u, 0)
                e_down(u - 1, 1)
                e_turn(u, 1)
                e_th(u, 0)
                e_gu(u, 1)
                e_down(u, 0)
                e_turn(u + 1, 0)
                e_th(u, 1)
            u = NE // 2 - 1
            e_gu(u, 0)
            e_down(u - 1, 1)
            e_turn(u, 1)
            e_th(u, 0)
            e_gu(u, 1)
            e_down(u, 0)
            e_th(u, 1)
            e_down(u, 1)
            pe.wait_ge(route_ctrl, 2)
            pe.wait_ge(ye_act, NE)
            pe.wait_ge(ye_dve, NE)
            n_ov = pe.value_load(ctrl_i[0:1, 31:32], min_val=0, max_val=NOV)
            with pe.Fori(0, NOV) as o:
                with pe.If(n_ov > o):
                    turn_rows(0, ov["gather"], 16 * o + 16, None, None, ov["xtr"])
                    gate_up(0, ov["xe"], o + 1, ov["w"], 32 * o + 32, ov["gu"])
                    turn_hidden(0, ov["hid"], o + 1, ov["htr"])
                    down(0, ov["hidT"], o + 1, ov["w"], 32 * o + 32, [], ov["dn"])

            for c in range(KD):
                pe.wait_ge(norm_ready, NORM["h2"] + 4)
                turn("hT2", c, [tm(hid2, t)[:, c * P:(c + 1) * P] for t in range(NT)])
            evac("hT2", 7)
            for i in range(8):
                t, half = i // 2, i % 2
                if i == 0:
                    for k in range(KD):
                        need("uv", k)
                product("uv", i, [fm(h2T, k)[:, t * P:(t + 1) * P] for k in range(KD)],
                        [panel("uv", k)[:, half * 512:half * 512 + 512] for k in range(KD)])
            for name, n in (("zq", 4), ("kc", 2), ("ksw", 2)):
                for c in range(n):
                    need(name, c)
                    product(name, c, mcols(name, c, KD), [fm(h2T, k) for k in range(KD)])
            for t in range(NT):
                if t == 0:
                    for k in range(4):
                        need("vs", k)
                product("vs", t, [fm(h2T, k)[:, t * P:(t + 1) * P] for k in range(KD)],
                        [panel("vs", k // 2)[:, (k % 2) * 512:(k % 2) * 512 + 280] for k in range(KD)],
                        tile("vs", t)[:, 0:280])
            pe.wait_ge(ws_masked, 1)
            pe.wait_ge(vhat_ready, 4)
            for h in range(8):
                product("sv", h, [wsT[:, h, :]], [vg[:, :, 64 * h:64 * h + 64]],
                        tile("sv", h)[:, 0:256].rearrange("p (c d) -> p c d", c=4))
            evac("kc", 1)
            for what, name, x, pos, j0 in (("w1k", "ck", kcA, "pos_k", 0), ("w1v", "ck", vcA, "pos_v", 2)):
                for k in range(4):
                    need(what, k)
                for jt in range(2):
                    free(name, j0 + jt)
                    dst = tile(name, j0 + jt)
                    w1 = [panel(what, i // 4)[:, (i % 4) * 256 + jt * P:(i % 4) * 256 + jt * P + P] for i in range(16)]
                    for i in range(16):
                        nc.tensor.matmul(dst[:, 0:62].rearrange("p (j n) -> p j n", j=2), w1[i],
                                         x[:, :, i:i + 16 * (NC_ - 1) + 1:16], start=(i == 0), stop=(i == 15))
                    for i in range(16):
                        mm = nc.tensor.matmul(dst[:, 62:63], w1[i], col(pos, i), start=(i == 0), stop=(i == 15))
                    close(mm, name, j0 + jt)
            pe.wait_ge(in_misc, 64)
            evac("ck", 1)
            free("kcc", 0)
            for j in range(2):
                for c in range(2):
                    mm = nc.tensor.matmul(tile("kcc", 0)[64 * j:64 * j + 64, 0:NC_], cmpw2[:, 0, c, :],
                                          h1k[:, c, 32 * j:32 * j + NC_], start=(c == 0), stop=(c == 1))
            close(mm, "kcc", 0)
            evac("ck", 3)
            free("vcc", 0)
            for j in range(2):
                for i in range(4):
                    for c in range(2):
                        mm = nc.tensor.matmul(tile("vcc", 0)[32 * i:32 * i + 32, 64 * j:64 * j + 64],
                                              h1v[:, c, 32 * j:32 * j + 32], cmpw2[:, 1, c, :], start=(c == 0), stop=(c == 1))
            close(mm, "vcc", 0)
            evac("kcc", 0)
            for qt in range(NT):
                free("sc", qt)
                dst = tile("sc", qt)[:, 0:256].rearrange("p (j i n) -> p j i n", j=2, i=4)
                for i in range(4):
                    mm = nc.tensor.matmul(dst[:, :, i, :], fm(q2T, i)[:, qt * P:(qt + 1) * P], kcT, start=True, stop=True)
                close(mm, "sc", qt)
            evac("sv", 7)
            for c in range(4):
                turn("aT", c, [ug[:, t, c * P:(c + 1) * P] for t in range(NT)])
            for k in range(4):
                need("woa", k)
            evac("aT", 3)
            for i in range(8):
                t, half = i // 2, i % 2
                product("woa", i, [fm(aT, k)[:, t * P:(t + 1) * P] for k in range(4)],
                        [panel("woa", k)[:, half * 512:half * 512 + 512] for k in range(4)])
            for qt in range(NT):
                pe.wait_ge(cmp_exp, NT + qt + 1)
                turn("pct", qt, [scs[:, qt, 4 * j:4 * j + 4, :].rearrange("p h n -> p (h n)") for j in range(2)])
            for w in range(NV2 + 2):
                if w < NV2:
                    g, br = w // 2, w % 2
                    r = slice(64 * (g // 4), 64 * (g // 4) + 64)
                    for qt in range(NT):
                        product("s2", 4 * w + qt, [fm(q2T, g % 4)[r, qt * P:(qt + 1) * P]],
                                [(ksT, kwT)[br][r, 0:(qt + 1) * P]], tile("s2", 4 * w + qt)[:, 0:(qt + 1) * P])
                if 1 <= w <= NV2:
                    for qt in range(NT):
                        n = 4 * (w - 1) + qt
                        pe.wait_ge(probs_ready, 48 + n + 1)
                        turn("pt2", n, [probs(w - 1, qt)[:, k * P:(k + 1) * P] for k in range(qt + 1)])
                if w >= 3 and w % 2 == 1:
                    values2((w - 3) // 2)
            evac("o2", 7)
            free("sb", 0)
            for t in range(NT):
                for c in range(4):
                    mm = nc.tensor.matmul(tile("sb", 0)[:, t:t + 1], bsq[:, c * T + t * P:c * T + (t + 1) * P],
                                          ones_f[:, 0:1], start=(c == 0), stop=(c == 3))
            close(mm, "sb", 0)
            for i in range(8):
                t, half = i // 2, i % 2
                if i == 0:
                    for k in range(4):
                        need("wob", k)
                product("wob", i, [fm(bT, k)[:, t * P:(t + 1) * P] for k in range(4)],
                        [panel("wob", k)[:, half * 512:half * 512 + 512] for k in range(4)])
            for c in range(KD):
                pe.wait_ge(norm_ready, NORM["h4"] + 4)
                turn("h4T", c, [tm(h4, t)[:, c * P:(c + 1) * P] for t in range(NT)])
            evac("h4T", 6)
            evac("h4T", 7)
            for f in range(FT):
                for name in ("fg", "fu"):
                    need(name, f)
                    product(name, f, mcols(name, f, KD), [fm(h4T, k) for k in range(KD)])
            evac("fu", FT - 1)
            for half in range(2):
                for t in range(NT):
                    free("fd", 4 * half + t)
                for k in range(FT):
                    n = 11 * half + k // 2
                    if k % 2 == 0:
                        need("fd", n)
                    for t in range(NT):
                        mm = nc.tensor.matmul(tile("fd", 4 * half + t)[:, :], actf[k][:, t * P:(t + 1) * P],
                                              panel("fd", n)[:, (k % 2) * 512:(k % 2) * 512 + 512],
                                              start=(k == 0), stop=(k == FT - 1))
                        if k == FT - 1:
                            close(mm, "fd", 4 * half + t)
                        elif k % 2 == 1 and t == NT - 1:
                            mm.then_inc(ffn_used, 1)
            assert closed[0] == plan.total

        @block.scalar
        def _(act):
            def full(name, i):
                act.wait_ge(psum_full, plan.full(name, i))

            def copy(name, i, dst, src, scale=1.0):
                full(name, i)
                nc.scalar.activation(dst, src, ACT.Copy, scale=scale).then_inc(act_evac, 1)

            def s5_tables(i):
                act.wait_ge(s5_frac, i + 1)
                if i >= 2:
                    act.wait_ge(s5_x, i - 1)
                c, s = s5cos[i % 2], s5sin[i % 2]
                nc.scalar.activation(c, s5f, ACT.Abs).then_inc(act_step, 1)
                astep[0] += 1
                nc.scalar.activation(s, s5f, ACT.Sin, scale=SIN_SCALE)
                act.wait_ge(act_step, astep[0])
                nc.scalar.activation(c, c, ACT.Sin, scale=-SIN_SCALE, bias=half_pi).then_inc(s5_tab, 1)

            astep = [0]

            def exp(name, n, m, dst, width, freed):
                act.wait_ge(max_ready, m + 1)
                if freed:
                    full(*freed)
                nc.scalar.activation(dst, tile(name, n)[:, 0:width], ACT.Exp, bias=nmax[:, m % 4:m % 4 + 1],
                                     accum_out=rsum[:, m % 4:m % 4 + 1]).then_inc(act_evac, 1)

            def sum_squares(src, dst, junk):
                nc.scalar.activation(junk, src, ACT.Square, accum_out=dst)

            act.dma_start(rope_k.bitcast(I32), a["positions"].broadcast_to([P, T])).then_inc(in_pos, 16)
            act.wait_ge(in_const, 32)
            act.wait_ge(pool_init, 1)
            dt, ardt, cth, sth, absf = s5tmp[:, 0:16], s5tmp[:, 16:32], s5tmp[:, 64:80], s5tmp[:, 80:96], s5tmp[:, 208:224]
            nc.scalar.activation(dt, colr("log_dt"), ACT.Exp).then_inc(s5_c, 1)
            act.wait_ge(s5_phi, 1)
            nc.scalar.activation(mag, ardt, ACT.Exp).then_inc(s5_c, 1)
            nc.scalar.activation(sth, phi, ACT.Sin, scale=SIN_SCALE).then_inc(s5_c, 1)
            nc.scalar.activation(absf, phi, ACT.Abs).then_inc(act_step, 1)
            act.wait_ge(act_step, 1)
            nc.scalar.activation(cth, absf, ACT.Sin, scale=-SIN_SCALE, bias=half_pi).then_inc(s5_c, 1)
            astep[0] = 1
            act.wait_ge(rope_arg, 2)
            nc.scalar.activation(rope_q[:, :], rope_q[:, :], ACT.Sin, scale=col("sign", 0)).then_inc(rope_tab, 1)
            nc.scalar.activation(rope_k, rope_k, ACT.Sin, scale=col("sign", 1)).then_inc(rope_tab, 1)
            s5_tables(0)
            for i in range(4):
                copy("u", i, fm(uT, i), tile("u", i)[:, :])
            for t in range(NT):
                copy("hqkv", t, hq[:, t, :], tile("hqkv", t)[:, :])
                act.wait_ge(act_evac, plan.done("hqkv", t))
                for b in range(2):
                    nc.scalar.activation(fm(hT, 2 * (t % 2) + b)[:, 0:256], hq[:, t, 256 * b:256 * b + 256], ACT.Square,
                                         accum_out=sumsq[:, 2 * t + b:2 * t + b + 1]).then_inc(sumsq_ready, 1)
                    act.wait_ge(sumsq_ready, 2 * t + b + 1)
                if t < 3:
                    s5_tables(t + 1)
            for c in range(4):
                g = col("q_norm_g", c) if c < 2 else col("kv_norm_g", c - 2)
                copy("hT", c, fm(hT, c), tile("hT", c)[:, :], g)
            for i in range(4, 7):
                s5_tables(i)
            for c in range(4):
                full("kn", c)
                nc.scalar.activation(fm(khat, 2 * c)[0:64, :], tile("kn", c)[0:64, :], ACT.Copy)
                nc.scalar.activation(fm(khat, 2 * c + 1)[0:64, :], tile("kn", c)[64:128, :], ACT.Copy).then_inc(act_evac, 1)
            for t in range(NT):
                copy("v", t, v_tok[:, t, :], tile("v", t)[:, :])
            for h in range(H1 + 2):
                if h < H1:
                    for qt in range(NT):
                        exp("s", 4 * h + qt, 4 * h + qt, probs(h, qt), (qt + 1) * P,
                            ("pt", 4 * (h - 2) + qt) if h >= 2 else None)
                if h >= 2:
                    g = h - 2
                    r = slice(64 * (g % 2), 64 * (g % 2) + 64)
                    copy("o", g, fm(oT, g // 2)[r, :], tile("o", g)[r, :])
                if h <= H1:
                    s5_tables(7 + h)
                if 1 <= h <= H1:
                    g = h - 1
                    for qt in (1, 3):
                        full("pt", 4 * g + qt)
                        if g >= 2:
                            full("o", g - 2)
                        nc.scalar.activation(probsT(g)[:, 0:qt + 1, qt * P:(qt + 1) * P],
                                             tile("pt", 4 * g + qt)[:, 0:(qt + 1) * P].rearrange("p (k n) -> p k n", n=P),
                                             ACT.Copy).then_inc(act_evac, 1)
            for j in range(3):
                act.wait_ge(y_ready, j + 1)
                nc.scalar.activation(fm(yT, j), fm(yT, j), ACT.Gelu_apprx_tanh).then_inc(gelu_ready, 1)
            for m in range(KD):
                full("gm", m)
                if m >= 2:
                    act.wait_ge(merged_ready, m - 1)
                nc.scalar.activation(sig_a[m % 2], tile("gm", m)[:, :], ACT.Sigmoid).then_inc(act_evac, 1)
            act.wait_ge(y_ready, 4)
            nc.scalar.activation(fm(yT, 3), fm(yT, 3), ACT.Gelu_apprx_tanh).then_inc(gelu_ready, 1)
            act.dma_start(gb[:, 0:D], a["rows"][0:1, :].broadcast_to([P, D])).then_inc(in_ln, 16)
            act.dma_start(gb[:, D:2 * D], a["rows"][1:2, :].broadcast_to([P, D])).then_inc(in_ln, 16)
            act.dma_start(xtok[:, :], a["x_tm"]).then_inc(in_xtok, 16)
            for t in range(2):
                act.dma_start(memtok[t], a["mem"][t * P:(t + 1) * P, :]).then_inc(in_mem, 16)
            act.dma_start(s5x[:, 0:512], a["w_router"]).then_inc(in_misc, 16)
            act.dma_start(s5x[:, 512:768], a["cmp_w2"]).then_inc(in_misc, 16)
            act.dma_start(gate_b, a["rows"][8:9, 0:24].broadcast_to([P, 24])).then_inc(in_misc, 16)
            act.dma_start(rt_bias, a["rows"][9:10, 0:64].broadcast_to([P, 64])).then_inc(in_misc, 16)
            for m in range(KD):
                full("gs", m)
                act.wait_ge(merged_ready, KD + max(0, m - 1))
                nc.scalar.activation(sig_a[m % 2], tile("gs", m)[:, :], ACT.Sigmoid).then_inc(act_evac, 1)
                full("gate", m)
                nc.scalar.activation(sig_b[m % 2], tile("gate", m)[:, :], ACT.Sigmoid).then_inc(act_evac, 1)
                if m >= 4:
                    c = m - 4
                    full("memT", c)
                    for j in range(2):
                        k = 2 * c + j
                        i = nc.scalar.activation(memT[:, k * 256:(k + 1) * 256], tile("memT", c)[:, 256 * j:256 * j + 256],
                                                 ACT.Identity, scale=col("mem_g", k), bias=col("mem_b", k))
                    i.then_inc(act_evac, 1)
            for h in range(XH):
                copy("kx", h, kxT[:, h, :], tile("kx", h)[:, 0:256])
            for t in range(2):
                copy("vx", t, vx[:, t, :], tile("vx", t)[:, :])
            for c in range(1, KD, 2):
                copy("x1T", c, fm(x1T, c), tile("x1T", c)[:, :])
            act.wait_ge(norm_ready, NORM["ln1"] + 4)
            for j in range(2):
                act.dma_start(gb[:, j * D:(j + 1) * D], a["rows"][2 + j:3 + j, :].broadcast_to([P, D])).then_inc(in_ln, 16)
            for h in range(XH):
                copy("xq", h, fm(xqT, h), tile("xq", h)[:, :], XD ** -0.5)
            for h in range(XH + 2):
                if h < XH:
                    for qt in range(NT):
                        exp("xs", 4 * h + qt, 32 + 4 * h + qt, xprobs(h, qt), 256,
                            ("xpt", 4 * (h - 2) + qt) if h >= 2 else None)
                if h >= 2:
                    copy("xo", h - 2, fm(oxT, h - 2), tile("xo", h - 2)[:, :])
                if 1 <= h <= XH:
                    g = h - 1
                    for qt in (1, 3):
                        full("xpt", 4 * g + qt)
                        if g >= 2:
                            full("xo", g - 2)
                        nc.scalar.activation(probsT(g)[:, 0:2, qt * P:(qt + 1) * P],
                                             tile("xpt", 4 * g + qt)[:, 0:256].rearrange("p (k n) -> p k n", n=P),
                                             ACT.Copy).then_inc(act_evac, 1)
            act.wait_ge(norm_ready, NORM["ln2"] + 4)
            for t in range(NT):
                act.dma_start(scratch["x2"][t * P:(t + 1) * P, :], tm(x2, t)).then_inc(x2_stored, 16)
            for j in range(2):
                act.dma_start(gb[:, j * D:(j + 1) * D], a["rows"][4 + j:5 + j, :].broadcast_to([P, D])).then_inc(in_ln, 16)
            for c in range(1, KD, 2):
                copy("x2T", c, fm(x2T, c), tile("x2T", c)[:, :])
            for t in range(NT):
                full("lg", t)
                nc.scalar.activation(score[:, 64 * t:64 * t + 64], tile("lg", t)[:, 0:64], ACT.Sigmoid).then_inc(act_evac, 1)
            for c in range(2):
                full("sg", c)
                nc.scalar.activation(shsig[c], tile("sg", c)[:, :], ACT.Silu).then_inc(act_evac, 1)

            def x_copy(b, s_full, n_full, s_ready):
                act.wait_ge(s_full, n_full)
                for j in range(2):
                    i = nc.scalar.activation(xe[b][:, 4 * j:4 * j + 4, :],
                                             bank[j][:, :].rearrange("p (k n) -> p k n", n=P), ACT.Copy)
                i.then_inc(s_ready, 1)

            def silu(b, s_full, n_full, s_ready):
                act.wait_ge(s_full, n_full)
                nc.scalar.activation(gsilu[b], bank[2 + b][:, 0:256], ACT.Silu).then_inc(s_ready, 1)

            def y_copy(b, s_full, n_full, s_ready):
                act.wait_ge(s_full, n_full)
                nc.scalar.activation(ye[b][:, 0:512], bank[5][:, :], ACT.Copy).then_inc(s_ready, 1)

            def e_x(u, b):
                x_copy(b, xtr_full, 2 * u + b + 1, xe_ready)

            def e_silu(u, b, first=False):
                if not first:
                    act.wait_ge(hid_ready, 2 * u + b - 1)
                silu(b, gu_full, 2 * u + b + 1, silu_ready)

            def e_y(u, b, first=False):
                e = 2 * u + b
                if not first:
                    act.wait_ge(y_stored[b], 16 * u)
                y_copy(b, dn_full, e + 1, ye_act)
                act.wait_ge(ye_act, e + 1)
                act.wait_ge(ye_dve, e + 1)
                act.dma_start(scratch["y"][bass.ds(e * P, P), :], ye[b]).then_inc(y_stored[b], 16)

            e_x(0, 0)
            e_silu(0, 0, True)
            e_x(0, 1)
            e_silu(0, 1, True)
            e_y(0, 0, True)
            e_x(1, 0)
            e_silu(1, 0)
            e_y(0, 1, True)
            e_x(1, 1)
            e_silu(1, 1)
            e_y(1, 0)
            e_x(2, 0)
            with act.Fori(2, NE // 2 - 1) as u:
                e_silu(u, 0)
                e_y(u - 1, 1)
                e_x(u, 1)
                e_silu(u, 1)
                e_y(u, 0)
                e_x(u + 1, 0)
            u = NE // 2 - 1
            e_silu(u, 0)
            e_y(u - 1, 1)
            e_x(u, 1)
            e_silu(u, 1)
            e_y(u, 0)
            e_y(u, 1)
            act.wait_ge(route_ctrl, 2)
            for b in range(2):
                act.wait_ge(y_stored[b], 16 * NE // 2)
            n_ov = act.value_load(ctrl_i[0:1, 31:32], min_val=0, max_val=NOV)
            with act.Fori(0, NOV) as o:
                with act.If(n_ov > o):
                    x_copy(0, ov["xtr"], o + 1, ov["xe"])
                    silu(0, ov["gu"], o + 1, ov["silu"])
                    y_copy(0, ov["dn"], o + 1, ov["yact"])

            act.dma_start(wsT, a["gmlp_ws"]).then_inc(in_ln, 16)
            for c in range(KD):
                copy("hT2", c, fm(h2T, c), tile("hT2", c)[:, :], col("norm_mix", c))
            act.wait_ge(norm_ready, NORM["h2"] + 4)
            act.dma_start(gb[:, 0:512], a["rows"][7:8, 0:512].broadcast_to([P, 512])).then_inc(in_ln, 16)
            act.dma_start(gb[:, D:2 * D], a["rows"][6:7, :].broadcast_to([P, D])).then_inc(in_ln, 16)
            for i in range(8):
                t, half = i // 2, i % 2
                full("uv", i)
                nc.scalar.activation((ug, vg)[half][:, t, :], tile("uv", i)[:, :], ACT.Gelu_apprx_tanh).then_inc(act_evac, 1)
            act.wait_ge(act_evac, plan.done("uv", 7))
            for t in range(NT):
                nc.scalar.activation(slab9[:, 512 * t:512 * t + 512], vg[:, t, :], ACT.Square,
                                     accum_out=sumsq[:, t:t + 1]).then_inc(sumsq_ready, 1)
            for c in range(4):
                copy("zq", c, fm(q2T, c), tile("zq", c)[:, :], 64 ** -0.5)
            copy("ksw", 0, ksT, tile("ksw", 0)[:, :])
            copy("ksw", 1, kwT, tile("ksw", 1)[:, :])
            for t in range(NT):
                full("vs", t)
                nc.scalar.activation(vsw[:, t, :], tile("vs", t)[:, 0:256], ACT.Copy)
                nc.scalar.activation(gates[:, t, :], tile("vs", t)[:, 256:280], ACT.Copy).then_inc(act_evac, 1)
            act.wait_ge(cmp_ready, 1)
            nc.scalar.activation(gates, gates, ACT.Sigmoid).then_inc(act_ready, 1)
            for c in range(4):
                full("ck", c)
                nc.scalar.activation(cbias[:, c:c + 1], tile("ck", c)[:, 62:63], ACT.Copy).then_inc(act_step, 1)
                astep[0] += 1
                act.wait_ge(act_step, astep[0])
                dst = (h1k, h1v)[c // 2][:, c % 2, :].rearrange("p (j n) -> p j n", j=2)[:, :, 0:NC_]
                nc.scalar.activation(dst, tile("ck", c)[:, 0:62].rearrange("p (j n) -> p j n", j=2),
                                     ACT.Gelu_apprx_tanh, bias=cbias[:, c:c + 1]).then_inc(act_evac, 1)
            full("kcc", 0)
            for j in range(2):
                r = slice(64 * j, 64 * j + 64)
                i = nc.scalar.activation(kcT[r, j, 0:NC_], tile("kcc", 0)[r, 0:NC_], ACT.Copy)
            i.then_inc(act_evac, 1)
            copy("vcc", 0, vcR, tile("vcc", 0)[:, 0:128].rearrange("p (j n) -> p j n", j=2))
            for qt in range(NT):
                act.wait_ge(cmp_exp, qt + 1)
                nc.scalar.activation(scs[:, qt, :, 0:NC_], scs[:, qt, :, 0:NC_], ACT.Exp).then_inc(act_ready, 1)
            act.wait_ge(dve_evac, plan.done("sv", 7))
            for t in range(NT):
                nc.scalar.activation(vg[:, t, :], ug[:, t, :], ACT.Square,
                                     accum_out=sumsq[:, 4 + t:5 + t]).then_inc(sumsq_ready, 1)
            for c in range(4):
                copy("aT", c, fm(aT, c), tile("aT", c)[:, :], col("out_a", c))
            for w in range(NV2 + 2):
                if w < NV2:
                    for qt in range(NT):
                        exp("s2", 4 * w + qt, 48 + 4 * w + qt, probs(w, qt), (qt + 1) * P,
                            ("pt2", 4 * (w - 2) + qt) if w >= 2 else None)
                if 1 <= w <= NV2:
                    g = w - 1
                    for qt in (1, 3):
                        full("pt2", 4 * g + qt)
                        if g >= 2:
                            full("o2", g // 2 - 1)
                        nc.scalar.activation(probsT(g)[:, 0:qt + 1, qt * P:(qt + 1) * P],
                                             tile("pt2", 4 * g + qt)[:, 0:(qt + 1) * P].rearrange("p (k n) -> p k n", n=P),
                                             ACT.Copy).then_inc(act_evac, 1)
                if w >= 3 and w % 2 == 1:
                    g = (w - 3) // 2
                    full("o2", g)
                    r = slice(64 * (g % 2), 64 * (g % 2) + 64)
                    nc.scalar.activation(fm(bsq, g // 2)[r, :], tile("o2", g)[r, :], ACT.Square)
                    nc.scalar.activation(fm(bT, g // 2)[r, :], tile("o2", g)[r, :], ACT.Copy,
                                         scale=cols[r, COLS["out_b"][0] + g // 2:COLS["out_b"][0] + g // 2 + 1]).then_inc(act_evac, 1)

            for c in range(1, KD, 2):
                copy("h4T", c, fm(h4T, c), tile("h4T", c)[:, :], col("norm_ffn", c))
            for f in range(FT):
                full("fg", f)
                if f >= 2:
                    act.wait_ge(dve_evac, plan.done("fu", f - 2))
                nc.scalar.activation(fsilu[f % 2], tile("fg", f)[:, :], ACT.Silu).then_inc(act_evac, 1)

        @block.vector
        def _(dve):
            step = [0]
            asked = [0]

            def mark(ins):
                step[0] += 1
                ins.then_inc(dve_step, 1)
                return step[0]

            def link(ins):
                dve.wait_ge(dve_step, mark(ins))

            def full(name, i):
                dve.wait_ge(psum_full, plan.full(name, i))

            def ts(out_, in_, s1, s2, op0, op1=ALU.bypass):
                return nc.vector.tensor_scalar(out_, in_, s1, s2, op0, op1)

            def tt(out_, x, y, op):
                return nc.vector.tensor_tensor(out_, x, y, op)

            def stt(out_, x, s, y, op0, op1):
                return nc.vector.scalar_tensor_tensor(out_, x, s, y, op0, op1)

            def copy(name, i, dst, src):
                full(name, i)
                nc.vector.tensor_copy(dst, src).then_inc(dve_evac, 1)

            tmp = [s5tmp[:, 16 * k:16 * k + 16] for k in range(16)]
            dve.wait_ge(in_const, 32)
            dve.wait_ge(s5_c, 1)
            dt, ardt, th, k2, cth, sth, den, t0, t1, nr, cr, ci, ni, absf = tmp[:14]
            link(tt(ardt, colr("a_re"), dt, ALU.mult))
            link(tt(th, colr("a_im"), dt, ALU.mult))
            link(ts(k2, th, 1.0 / (2 * np.pi), MAGIC, ALU.mult, ALU.add))
            link(ts(k2, k2, MAGIC, None, ALU.subtract))
            link(stt(t0, k2, -TWO_PI_HI, th, ALU.mult, ALU.add))
            link(stt(t0, k2, -TWO_PI_LO, t0, ALU.mult, ALU.add))
            link(ts(phi, t0, 1.0 / (2 * np.pi), None, ALU.mult))
            link(ts(phi_hi, phi, MAGIC12, MAGIC12, ALU.add, ALU.subtract))
            link(stt(t1, phi_hi, -TWO_PI_HI, t0, ALU.mult, ALU.add))
            link(stt(t1, phi_hi, -TWO_PI_LO, t1, ALU.mult, ALU.add))
            link(ts(phi_lo, t1, 1.0 / (2 * np.pi), None, ALU.mult))
            link(ts(phi, phi, -0.5, 0.5, ALU.max, ALU.min))
            nc.vector.tensor_copy(absf, ardt).then_inc(s5_phi, 1)

            dve.wait_ge(in_pos, 16)
            link(nc.vector.tensor_copy(rope_k, rope_k.bitcast(I32)))
            for b, dst in ((0, rope_q[:, :]), (1, rope_k)):
                link(ts(krope, rope_k, col("freq", b), None, ALU.mult))
                link(ts(tiny[:, 0:1], col("phase", b), 0.25, None, ALU.mult))
                link(ts(krope_t, krope, 1.0 / (2 * np.pi), tiny[:, 0:1], ALU.mult, ALU.add))
                link(ts(krope_t, krope_t, MAGIC, None, ALU.add))
                link(ts(krope_t, krope_t, MAGIC, None, ALU.subtract))
                link(stt(krope, krope_t, -TWO_PI_HI, krope, ALU.mult, ALU.add))
                link(stt(krope, krope_t, -TWO_PI_LO, krope, ALU.mult, ALU.add))
                link(ts(tiny[:, 1:2], col("phase", b), np.pi / 2, None, ALU.mult))
                link(ts(krope, krope, tiny[:, 1:2], PI_LIM, ALU.add, ALU.min))
                ts(dst, krope, -PI_LIM, None, ALU.max).then_inc(rope_arg, 1)
                dve.wait_ge(rope_arg, b + 1)

            def s5_turns(i):
                dve.wait_ge(s5_uk_sem, i + 1)
                if i >= 1:
                    dve.wait_ge(s5_tab, i)
                link(stt(s5k, s5k, MAGIC, s5u, ALU.subtract, ALU.subtract))
                link(stt(s5f, iota_t[:, :], phi_lo[:, i:i + 1], s5k, ALU.mult, ALU.subtract))
                ts(s5f, s5f, -0.5, 0.5, ALU.max, ALU.min).then_inc(s5_frac, 1)

            def s5_core(i):
                dve.wait_ge(s5_tab, i + 1)
                c, s = s5cos[i % 2], s5sin[i % 2]
                zr, zi = s5zr[i % 2], s5zi[i % 2]
                if i + 1 < NST:
                    s5_turns(i + 1)
                if i >= 2:
                    dve.wait_ge(s5_x, i - 1)
                full("s5r", i)
                tt(s5wr, tile("s5r", i)[:, :], c, ALU.mult)
                tt(zr, tile("s5r", i)[:, :], s, ALU.mult).then_inc(dve_evac, 1)
                full("s5i", i)
                tt(s5wi, tile("s5i", i)[:, :], c, ALU.mult)
                tt(zi, tile("s5i", i)[:, :], s, ALU.mult).then_inc(dve_evac, 1)
                dve.wait_ge(dve_evac, plan.done("s5i", i))
                tt(s5wr, s5wr, zi, ALU.add)
                link(tt(s5wi, s5wi, zr, ALU.subtract))
                m = mag[:, i:i + 1].broadcast_to([P, T])
                nc.vector.tensor_tensor_scan(zr, m, s5wr, 0.0, ALU.mult, ALU.add)
                nc.vector.tensor_tensor_scan(zi, m, s5wi, 0.0, ALU.mult, ALU.add).then_inc(s5_z, 1)

            def s5_y(j):
                full("s5y", j)
                if j >= 0:
                    stt(fm(yT, j), fm(uT, j), col("s5_d", j), tile("s5y", j)[:, :], ALU.mult, ALU.add).then_inc(dve_evac, 1)
                dve.wait_ge(dve_evac, plan.done("s5y", j))
                nc.vector.tensor_copy(tiny[:, 2:3], tiny[:, 0:1]).then_inc(y_ready, 1)

            def root(src, scale, eps):
                at, w = REQUESTS[asked[0]]
                asked[0] += 1
                ts(var[:, at:at + w], src, scale, eps, ALU.mult, ALU.add).then_inc(var_ready, 1)
                return rstd[:, at:at + w], asked[0]

            def moments(x0, x1, k):
                if x1 is None:
                    raise ValueError
                nc.vector.bn_stats(stats[:, 0:6], x0)
                link(nc.vector.bn_stats(stats[:, 6:12], x1))
                link(nc.vector.bn_aggr(mv[:, 2 * k:2 * k + 2], stats[:, 0:12]))

            def layer_norm(x, k, name, t, base, affine):
                r, n = pending[k]
                dve.wait_ge(rstd_ready, n)
                s = shift[:, k:k + 1]
                link(ts(s, mv[:, 2 * k:2 * k + 1], r, -1.0, ALU.mult, ALU.mult))
                last = ts(x, x, r, s, ALU.mult, ALU.add)
                if affine:
                    link(last)
                    link(tt(x, x, gb[:, 0:D], ALU.mult))
                    last = tt(x, x, gb[:, D:2 * D], ALU.add)
                return last

            pending = {}

            def ask_ln(x, k):
                moments(x[:, 0:512], x[:, 512:1024], k)
                pending[k] = root(mv[:, 2 * k + 1:2 * k + 2], 1.0, 1e-5)

            def ask_rms(x, k):
                moments(x[:, 0:512], x[:, 512:1024], k)
                m, q = mv[:, 2 * k:2 * k + 1], mv[:, 2 * k + 1:2 * k + 2]
                link(stt(q, m, m, q, ALU.mult, ALU.add))
                pending[k] = root(q, 1.0, 1e-6)

            dve.wait_ge(rope_tab, 1)
            link(ts(rope_q[:, :], rope_q[:, :], float(np.float32((NOPE + ROPE) ** -0.5)), None, ALU.mult))
            link(nc.vector.memset(rope_q[0:64, :], float(np.float32((NOPE + ROPE) ** -0.5))))
            s5_turns(0)
            dve.wait_ge(s5_c, 4)
            link(tt(cth, cth, mag, ALU.mult))
            link(tt(sth, sth, mag, ALU.mult))
            link(ts(nr, cth, 1.0, None, ALU.subtract))
            a_re, a_im = colr("a_re"), colr("a_im")
            link(tt(den, a_re, a_re, ALU.mult))
            link(tt(t0, a_im, a_im, ALU.mult))
            link(tt(den, den, t0, ALU.add))
            link(nc.vector.reciprocal(den, den))
            link(tt(t0, nr, a_re, ALU.mult))
            link(tt(t1, sth, a_im, ALU.mult))
            link(tt(cr, t0, t1, ALU.add))
            link(tt(cr, cr, den, ALU.mult))
            link(tt(t0, sth, a_re, ALU.mult))
            link(tt(t1, nr, a_im, ALU.mult))
            link(tt(ci, t0, t1, ALU.subtract))
            link(tt(ci, ci, den, ALU.mult))
            dve.wait_ge(in_s5, 16)
            crb, cib = [x.unsqueeze(2).broadcast_to([P, NST, 32]) for x in (cr, ci)]
            p0, p1, p2 = [u.rearrange("p (i n) -> p i n", i=NST) for u in (s5wr, s5wi, s5zr[0])]
            link(tt(p0, c_re, cib, ALU.mult))
            link(tt(p1, c_im, cib, ALU.mult))
            link(tt(p2, c_im, crb, ALU.mult))
            link(tt(c_re, c_re, crb, ALU.mult))
            link(tt(c_re, c_re, p1, ALU.subtract))
            link(tt(p0, p0, p2, ALU.add))
            link(ts(c_im, p0, -1.0, None, ALU.mult))
            for i in range(3):
                s5_core(i)
            dve.wait_ge(sumsq_ready, 8)
            dve.wait_ge(act_evac, plan.done("hqkv", 3))
            r8, n = root(sumsq, 1.0 / 256, 1e-6)
            dve.wait_ge(rstd_ready, n)
            for t in range(NT):
                ts(hq[:, t, 0:256], hq[:, t, 0:256], r8[:, 2 * t:2 * t + 1], None, ALU.mult)
                ts(hq[:, t, 256:512], hq[:, t, 256:512], r8[:, 2 * t + 1:2 * t + 2], None, ALU.mult).then_inc(norm_ready, 1)
            s5_core(3)
            dve.wait_ge(rope_tab, 2)
            full("krope", 0)
            tt(krope[64:128, :], tile("krope", 0)[0:64, :], rope_k[0:64, :], ALU.mult)
            tt(krope_t[64:128, :], tile("krope", 0)[64:128, :], rope_k[64:128, :], ALU.mult).then_inc(dve_evac, 1)
            dve.wait_ge(dve_evac, plan.done("krope", 0))
            tt(krope[64:128, :], krope[64:128, :], krope_t[64:128, :], ALU.add).then_inc(krope_ready, 1)
            for h in range(H1):
                full("q", h)
                tt(fm(qhat, h), tile("q", h)[:, :], rope_q[:, :], ALU.mult).then_inc(dve_evac, 1)
                if h in (1, 3, 5):
                    s5_core(4 + h // 2)

            def softmax_max(name, i, m, width, causal):
                full(name, i)
                if causal:
                    d = tile(name, i)[:, width - P:width]
                    link(tt(d, d, cst("causal"), ALU.add))
                nc.vector.tensor_reduce(nmax[:, m % 4:m % 4 + 1], tile(name, i)[:, 0:width], AX, ALU.max,
                                        negate=True).then_inc(max_ready, 1)

            def softmax_scale(name, i, m, p, gate=None):
                dve.wait_ge(act_evac, plan.done(name, i))
                c = slice(m % 4, m % 4 + 1)
                link(nc.vector.reciprocal(rinv[:, c], rsum[:, c]))
                f = rinv[:, c]
                if gate is not None:
                    link(tt(fac[:, c], rinv[:, c], gate, ALU.mult))
                    f = fac[:, c]
                ts(p, p, f, None, ALU.mult).then_inc(probs_ready, 1)

            def turned(name, i, g, qt, width, out_name, out_i):
                full(name, i)
                if out_name:
                    full(out_name, out_i)
                k = width // P
                nc.vector.tensor_copy(probsT(g)[:, 0:k, qt * P:(qt + 1) * P],
                                      tile(name, i)[:, 0:width].rearrange("p (k n) -> p k n", n=P)).then_inc(dve_evac, 1)

            for h in range(H1 + 2):
                if h < H1:
                    for qt in range(NT):
                        softmax_max("s", 4 * h + qt, 4 * h + qt, (qt + 1) * P, True)
                if h <= H1:
                    s5_core(7 + h)
                if h % 4 == 0 and 0 <= h // 4 < 3:
                    s5_y(h // 4)
                if 1 <= h <= H1:
                    g = h - 1
                    for qt in (0, 2):
                        turned("pt", 4 * g + qt, g, qt, (qt + 1) * P, "o" if g >= 2 else None, g - 2)
                if h < H1:
                    for qt in range(NT):
                        softmax_scale("s", 4 * h + qt, 4 * h + qt, probs(h, qt))
            for m in range(KD):
                full("ym", m)
                dve.wait_ge(act_evac, plan.done("gm", m))
                tt(fm(merged, m), tile("ym", m)[:, :], sig_a[m % 2], ALU.mult).then_inc(dve_evac, 1)
                dve.wait_ge(dve_evac, plan.done("ym", m))
                nc.vector.tensor_copy(tiny[:, 3:4], tiny[:, 0:1]).then_inc(merged_ready, 1)
                if m == 2:
                    s5_y(3)
            for m in range(KD):
                full("val", m)
                dve.wait_ge(act_evac, plan.done("gate", m))
                tt(gated[m % 2], tile("val", m)[:, :], sig_b[m % 2], ALU.mult).then_inc(dve_evac, 1)
                dve.wait_ge(dve_evac, plan.done("val", m))
                link(tt(gated[m % 2], gated[m % 2], sig_a[m % 2], ALU.mult))
                tt(fm(merged, m), fm(merged, m), gated[m % 2], ALU.add).then_inc(merged_ready, 1)
                if m == 2:
                    dve.wait_ge(in_mem, 32)
                    for t in range(2):
                        ask_ln(memtok[t], t)
                    for t in range(2):
                        layer_norm(memtok[t], t, "mem", t, 0, False).then_inc(norm_ready, 1)

            def residual(name, dst, res, alpha_first=True):
                for t in range(NT):
                    for half in range(2):
                        i = 2 * t + half
                        full(name, i)
                        h_ = slice(half * 512, half * 512 + 512)
                        stt(tm(dst, t)[:, h_], tm(res, t)[:, h_], ALPHA, tile(name, i)[:, :], ALU.mult, ALU.add).then_inc(dve_evac, 1)
                    dve.wait_ge(dve_evac, plan.done(name, 2 * t + 1))
                    yield t

            dve.wait_ge(in_xtok, 16)
            dve.wait_ge(in_ln, 32)
            for t in residual("mix", x1, xtok):
                ask_ln(tm(x1, t), t)
                if t >= 1:
                    layer_norm(tm(x1, t - 1), t - 1, "ln1", t - 1, 0, True).then_inc(norm_ready, 1)
            layer_norm(tm(x1, 3), 3, "ln1", 3, 0, True).then_inc(norm_ready, 1)
            for c in range(0, KD, 2):
                copy("x1T", c, fm(x1T, c), tile("x1T", c)[:, :])
            for h in range(XH + 1):
                if h < XH:
                    for qt in range(NT):
                        softmax_max("xs", 4 * h + qt, 32 + 4 * h + qt, 256, False)
                if 1 <= h <= XH:
                    g = h - 1
                    for qt in (0, 2):
                        turned("xpt", 4 * g + qt, g, qt, 256, "xo" if g >= 2 else None, g - 2)
                if h < XH:
                    for qt in range(NT):
                        softmax_scale("xs", 4 * h + qt, 32 + 4 * h + qt, xprobs(h, qt))
            dve.wait_ge(in_ln, 64)
            for t in residual("xa", x2, x1):
                ask_ln(tm(x2, t), t)
                if t >= 1:
                    layer_norm(tm(x2, t - 1), t - 1, "ln2", t - 1, 0, True).then_inc(norm_ready, 1)
            layer_norm(tm(x2, 3), 3, "ln2", 3, 0, True).then_inc(norm_ready, 1)
            for c in range(0, KD, 2):
                copy("x2T", c, fm(x2T, c), tile("x2T", c)[:, :])

            dve.wait_ge(in_misc, 64)
            dve.wait_ge(act_evac, plan.done("lg", 3))
            v3 = lambda x: x.rearrange("p (t e) -> p t e", t=4)
            link(tt(v3(sel), v3(score), rt_bias.unsqueeze(1).broadcast_to([P, 4, 64]), ALU.add))
            for g in range(32):
                i = nc.vector.max(top2[:, 8 * g:8 * g + 8], sel[:, 8 * g:8 * g + 8])
            link(i)
            t2 = top2.rearrange("p (g n) -> p g n", n=8)
            link(tt(gscore, t2[:, :, 0], t2[:, :, 1], ALU.add))
            for t in range(NT):
                gs = gscore[:, 8 * t:8 * t + 8]
                mine = gs.unsqueeze(2).broadcast_to([P, 8, 8])
                other = gs.unsqueeze(1).broadcast_to([P, 8, 8])
                ca, cb = [x.rearrange("p (g h) -> p g h", g=8) for x in (cmp_a, cmp_b)]
                link(tt(ca, other, mine, ALU.is_gt))
                link(tt(cb, other, mine, ALU.is_equal))
                link(tt(cmp_b, cmp_b, cst("gtri"), ALU.mult))
                link(tt(cmp_a, cmp_a, cmp_b, ALU.add))
                link(nc.vector.tensor_reduce(grank[:, 8 * t:8 * t + 8], ca, AX, ALU.add))
            link(ts(gkeep, grank, TOPG - 0.5, None, ALU.is_lt))
            link(ts(gpen, gkeep, BIG, -BIG, ALU.mult, ALU.add))
            v8 = lambda x: x.rearrange("p (g e) -> p g e", e=8)
            wide = lambda x: x.unsqueeze(2).broadcast_to([P, 32, 8])
            link(tt(v8(selm), v8(sel), wide(gkeep), ALU.mult))
            link(tt(v8(selm), v8(selm), wide(gpen), ALU.add))
            for t in range(NT):
                e = slice(64 * t, 64 * t + 64)
                k = slice(8 * t, 8 * t + 8)
                link(nc.vector.max(topv[:, k], selm[:, e]))
                link(nc.vector.max_index(topi[:, k].bitcast(U32), topv[:, k], selm[:, e]))
                link(nc.vector.match_replace(sel_rep[:, e], topv[:, k], selm[:, e], -3.0e38))
            link(nc.vector.tensor_copy(topf, topi.bitcast(U32)))
            tt(chosen, selm, sel_rep, ALU.is_gt).then_inc(route_mask, 1)
            for c in range(2):
                full("su", c)
                dve.wait_ge(act_evac, plan.done("sg", c))
                tt(actT[:, c * T:(c + 1) * T], tile("su", c)[:, :], shsig[c], ALU.mult).then_inc(dve_evac, 1)
            for t in residual("sd", acc, x2):
                pass
            full("pos", 0)
            nc.vector.tensor_copy(cnt, tile("pos", 0)[:, 256:320])
            nc.vector.tensor_copy(pos_sb, tile("pos", 0)[:, 0:256]).then_inc(dve_evac, 1)
            dve.wait_ge(dve_evac, plan.done("pos", 0))
            link(ts(ovn, cnt, 128.5, None, ALU.is_gt))
            for lim in (256.5, 384.5):
                link(stt(ovn, cnt, lim, ovn, ALU.is_gt, ALU.add))
            link(nc.vector.memset(cmp_a, 0.0))
            link(nc.vector.tensor_tensor_scan(ovincl, ovn, cmp_a, 0.0, ALU.add, ALU.add))
            link(tt(ovbase, ovincl, ovn, ALU.subtract))
            link(ts(q_blk, pos_sb, 127.5, None, ALU.is_gt))
            for lim in (255.5, 383.5):
                link(stt(q_blk, pos_sb, lim, q_blk, ALU.is_gt, ALU.add))
            link(stt(r_in, q_blk, -128.0, pos_sb, ALU.mult, ALU.add))
            iota = cst("iota64")
            b64 = lambda x: x.unsqueeze(1).broadcast_to([P, 4, 64])
            link(ts(cmp_b, ovbase, 63.0, None, ALU.add))
            link(tt(cmp_b, cmp_b, iota, ALU.subtract))
            link(tt(v3(t256), v3(q_blk), b64(cmp_b), ALU.add))
            link(ts(t256b, q_blk, 0.5, None, ALU.is_gt))
            link(tt(t256, t256, t256b, ALU.mult))
            link(tt(v3(blk), v3(t256), b64(iota), ALU.add))
            link(stt(addr, r_in, float(TABW), blk, ALU.mult, ALU.add))
            link(stt(yrow, blk, 128.0, r_in, ALU.mult, ALU.add))
            for t in range(NT):
                k = slice(8 * t, 8 * t + 8)
                oh, op = [x.rearrange("p (k e) -> p k e", k=8) for x in (onehot, oneprod)]
                link(tt(oh, iota.unsqueeze(1).broadcast_to([P, 8, 64]), topf[:, k].unsqueeze(2).broadcast_to([P, 8, 64]), ALU.is_equal))
                for src, dst in ((addr, addr_k), (yrow, yrow_k), (score, wk)):
                    link(tt(op, oh, src[:, 64 * t:64 * t + 64].unsqueeze(1).broadcast_to([P, 8, 64]), ALU.mult))
                    link(nc.vector.tensor_reduce(dst[:, k], op, AX, ALU.add))
            link(nc.vector.tensor_copy(tok_i[:, :], cst("tokid")))
            link(nc.vector.tensor_copy(yrow_i[:, :], yrow_k))
            nc.vector.tensor_copy(addr_i[:, :], addr_k).then_inc(route_addr, 1)
            w8 = wk.rearrange("p (t k) -> p t k", t=4)
            link(nc.vector.tensor_reduce(wsum, w8, AX, ALU.add))
            link(nc.vector.reciprocal(wsum, wsum))
            link(tt(w8, w8, wsum.unsqueeze(2).broadcast_to([P, 4, 8]), ALU.mult))
            link(ts(wk, wk, RSCALE, None, ALU.mult))
            bc = blk_cmp[0:1, :].rearrange("p (o e) -> p o e", o=32)
            link(tt(bc, ovincl[0:1, :].unsqueeze(1).broadcast_to([1, 32, 64]),
                    iota[0:1, 0:32].unsqueeze(2).broadcast_to([1, 32, 64]), ALU.is_le))
            link(nc.vector.tensor_reduce(blk_exp[0:1, :], bc, AX, ALU.add))
            link(ts(blk_exp[0:1, :], blk_exp[0:1, :], 63.0, None, ALU.min))
            nc.vector.tensor_copy(ctrl_i[0:1, 0:31], blk_exp[0:1, 0:31]).then_inc(route_ctrl, 1)
            nc.vector.tensor_copy(ctrl_i[0:1, 31:32], ovincl[0:1, 63:64]).then_inc(route_ctrl, 1)

            def hidden(b, s_silu, n_silu, s_ready):
                dve.wait_ge(s_silu, n_silu)
                tt(hid[b], bank[2 + b][:, 256:512], gsilu[b], ALU.mult).then_inc(s_ready, 1)

            def hidden_T(b, s_full, n_full, s_ready):
                dve.wait_ge(s_full, n_full)
                nc.vector.tensor_copy(hidT[b], bank[4][:, 0:256].rearrange("p (k n) -> p k n", k=2)).then_inc(s_ready, 1)

            def y_half(b, s_full, n_full, s_ready):
                dve.wait_ge(s_full, n_full)
                nc.vector.tensor_copy(ye[b][:, 512:1024], bank[6][:, :]).then_inc(s_ready, 1)

            def e_hid(u, b, first=False):
                if not first:
                    dve.wait_ge(htr_full, 2 * u + b - 1)
                hidden(b, silu_ready, 2 * u + b + 1, hid_ready)

            def e_hidT(u, b, first=False):
                if not first:
                    dve.wait_ge(dn_full, 2 * u + b - 1)
                hidden_T(b, htr_full, 2 * u + b + 1, hidT_ready)

            def e_y(u, b, first=False):
                if not first:
                    dve.wait_ge(y_stored[b], 16 * u)
                y_half(b, dn_full, 2 * u + b + 1, ye_dve)

            e_hid(0, 0, True)
            e_hidT(0, 0, True)
            e_hid(0, 1, True)
            e_y(0, 0, True)
            e_hidT(0, 1, True)
            e_hid(1, 0)
            e_y(0, 1, True)
            e_hidT(1, 0)
            e_hid(1, 1)
            e_y(1, 0)
            e_hidT(1, 1)
            with dve.Fori(2, NE // 2) as u:
                e_hid(u, 0)
                e_y(u - 1, 1)
                e_hidT(u, 0)
                e_hid(u, 1)
                e_y(u, 0)
                e_hidT(u, 1)
            e_y(NE // 2 - 1, 1)
            for b in range(2):
                dve.wait_ge(y_stored[b], 16 * NE // 2)
            n_ov = dve.value_load(ctrl_i[0:1, 31:32], min_val=0, max_val=NOV)
            with dve.Fori(0, NOV) as o:
                with dve.If(n_ov > o):
                    hidden(0, ov["silu"], o + 1, ov["hid"])
                    hidden_T(0, ov["htr"], o + 1, ov["hidT"])
                    y_half(0, ov["dn"], o + 1, ov["ydve"])
            for j in range(32):
                t = j // 8
                dve.wait_ge(ygot[j % 4], 16 * (j // 4) + 16)
                stt(tm(acc, t), ygath[j % 4], wk[:, j:j + 1], tm(acc, t), ALU.mult, ALU.add).then_inc(combined, 1)
                dve.wait_ge(combined, j + 1)
            dve.wait_ge(in_ln, 96)
            for t in range(NT):
                ask_ln(tm(acc, t), t)
            for t in range(NT):
                link(layer_norm(tm(acc, t), t, "ln3", t, 0, True))
                link(nc.vector.tensor_copy(tm(x3, t), tm(acc, t)))
            for t in range(NT):
                ask_rms(tm(x3, t), 4 + t)
            for t in range(NT):
                r, n = pending[4 + t]
                dve.wait_ge(rstd_ready, n)
                ts(tm(hid2, t), tm(x3, t), r, None, ALU.mult).then_inc(norm_ready, 1)
            dve.wait_ge(in_ln, 144)
            tt(wsT, wsT, cst("keep_ts").unsqueeze(1).broadcast_to([P, 8, P]), ALU.mult).then_inc(ws_masked, 1)
            dve.wait_ge(sumsq_ready, 8 + NT)
            rv, n = root(sumsq[:, 0:4], 1.0 / 512, 1e-6)
            dve.wait_ge(rstd_ready, n)
            for t in range(NT):
                stt(vg[:, t, :], vg[:, t, :], rv[:, t:t + 1], gb[:, 0:512], ALU.mult, ALU.mult).then_inc(vhat_ready, 1)
            link(nc.vector.memset(s5x[:, 1024:1344], 0.0))
            link(nc.vector.memset(scs, 0.0))
            ts(cneg, cst("cmp01"), 1.0, BIG, ALU.subtract, ALU.mult)
            for c, dst in ((0, kcA), (1, vcA)):
                full("kc", c)
                s = tile("kc", c)
                for j in range(2):
                    r = slice(64 * j, 64 * j + 64)
                    nc.vector.tensor_copy(dst[0:64, j, :], s[r, :])
                    i = nc.vector.tensor_copy(dst[64:128, j, 0:496], s[r, 16:512])
                i.then_inc(dve_evac, 1)
            dve.wait_ge(act_evac, plan.done("vs", 3))
            tt(gates, gates, gate_b.unsqueeze(1).broadcast_to([P, 4, 24]), ALU.add).then_inc(cmp_ready, 1)
            for h in range(8):
                full("sv", h)
                g = ug[:, :, 64 * h:64 * h + 64]
                stt(g, tile("sv", h)[:, 0:256].rearrange("p (c d) -> p c d", c=4), col("gmlp_bs", h), g,
                    ALU.add, ALU.mult).then_inc(dve_evac, 1)
            n01 = cst("cmp01").rearrange("p (t n) -> p t n", t=4)
            nneg = cneg.rearrange("p (t n) -> p t n", t=4)
            for qt in range(NT):
                full("sc", qt)
                x = scs[:, qt, :, 0:NC_]
                tt(x, tile("sc", qt)[:, 0:256].rearrange("p (h n) -> p h n", h=8)[:, :, 0:NC_],
                   nneg[:, qt:qt + 1, 0:NC_].broadcast_to([P, 8, NC_]), ALU.add).then_inc(dve_evac, 1)
                dve.wait_ge(dve_evac, plan.done("sc", qt))
                m = smax_c[:, 8 * qt:8 * qt + 8]
                link(nc.vector.tensor_reduce(m, x, AX, ALU.max))
                tt(x, x, m.unsqueeze(2).broadcast_to([P, 8, NC_]), ALU.subtract).then_inc(cmp_exp, 1)
            for qt in range(NT):
                dve.wait_ge(act_ready, 2 + qt)
                x = scs[:, qt, :, 0:NC_]
                m, f = ssum_c[:, 8 * qt:8 * qt + 8], fac_c[:, 8 * qt:8 * qt + 8]
                link(nc.vector.tensor_reduce(m, x, AX, ALU.add))
                link(nc.vector.reciprocal(m, m))
                link(tt(f, m, gates[:, qt, 0:8], ALU.mult))
                link(tt(x, x, f.unsqueeze(2).broadcast_to([P, 8, NC_]), ALU.mult))
                tt(x, x, n01[:, qt:qt + 1, 0:NC_].broadcast_to([P, 8, NC_]), ALU.mult).then_inc(cmp_exp, 1)
            dve.wait_ge(sumsq_ready, 8 + 2 * NT)
            ra, n = root(sumsq[:, 4:8], 1.0 / 512, 1e-6)
            dve.wait_ge(rstd_ready, n)
            for i in range(8):
                t, half = i // 2, i % 2
                full("woa", i)
                h_ = slice(half * 512, half * 512 + 512)
                stt(tm(x4, t)[:, h_], tile("woa", i)[:, :], ra[:, t:t + 1], tm(x3, t)[:, h_], ALU.mult, ALU.add).then_inc(dve_evac, 1)
            for qt in range(NT):
                full("pct", qt)
                nc.vector.tensor_copy(pcT[:, :, qt * P:(qt + 1) * P],
                                      tile("pct", qt)[:, 0:256].rearrange("p (j n) -> p j n", j=2)).then_inc(dve_evac, 1)
            for w in range(NV2 + 1):
                if w < NV2:
                    for qt in range(NT):
                        softmax_max("s2", 4 * w + qt, 48 + 4 * w + qt, (qt + 1) * P, True)
                if 1 <= w <= NV2:
                    g = w - 1
                    for qt in (0, 2):
                        turned("pt2", 4 * g + qt, g, qt, (qt + 1) * P, "o2" if g >= 2 else None, g // 2 - 1)
                if w < NV2:
                    for qt in range(NT):
                        c = 8 * (1 + w % 2) + w // 2
                        softmax_scale("s2", 4 * w + qt, 48 + 4 * w + qt, probs(w, qt), gates[:, qt, c:c + 1])
            full("sb", 0)
            nc.vector.tensor_copy(sumsq[:, 0:4], tile("sb", 0)[:, 0:4]).then_inc(dve_evac, 1)
            dve.wait_ge(dve_evac, plan.done("sb", 0))
            rb, n = root(sumsq[:, 0:4], 1.0 / 512, 1e-6)
            dve.wait_ge(rstd_ready, n)
            for t in range(NT):
                for half in range(2):
                    i = 2 * t + half
                    full("wob", i)
                    x = tm(x4, t)[:, half * 512:half * 512 + 512]
                    stt(x, tile("wob", i)[:, :], rb[:, t:t + 1], x, ALU.mult, ALU.add).then_inc(dve_evac, 1)
                dve.wait_ge(dve_evac, plan.done("wob", 2 * t + 1))
                ask_rms(tm(x4, t), t)
            for t in range(NT):
                r, n = pending[t]
                dve.wait_ge(rstd_ready, n)
                ts(tm(h4, t), tm(x4, t), r, None, ALU.mult).then_inc(norm_ready, 1)
            for c in range(0, KD, 2):
                full("h4T", c)
                ts(fm(h4T, c), tile("h4T", c)[:, :], col("norm_ffn", c), None, ALU.mult).then_inc(dve_evac, 1)
            for f in range(FT):
                full("fu", f)
                dve.wait_ge(act_evac, plan.done("fg", f))
                tt(actf[f], tile("fu", f)[:, :], fsilu[f % 2], ALU.mult).then_inc(dve_evac, 1)
            for half in range(2):
                for t in range(NT):
                    i = 4 * half + t
                    full("fd", i)
                    x = tm(x4, t)[:, half * 512:half * 512 + 512]
                    tt(x, tile("fd", i)[:, :], x, ALU.add).then_inc(dve_evac, 1)
                    if half == 1:
                        dve.wait_ge(dve_evac, plan.done("fd", i))
                        ask_rms(tm(x4, t), 4 + t)
            for t in range(NT):
                r, n = pending[4 + t]
                dve.wait_ge(rstd_ready, n)
                stt(tm(outb, t), tm(x4, t), r, gb[:, D:2 * D], ALU.mult, ALU.mult).then_inc(norm_ready, 1)
            assert asked[0] == len(REQUESTS)

        @block.gpsimd
        def _(pool):
            answered = [0]

            def answer(k=1):
                for _ in range(k):
                    at, w = REQUESTS[answered[0]]
                    answered[0] += 1
                    pool.wait_ge(var_ready, answered[0])
                    nc.gpsimd.tensor_tensor(rstd[:, at:at + w], var[:, at:at + w], minus_half[:, 0:w], ALU.pow).then_inc(rstd_ready, 1)

            psteps = [0]

            def link(ins):
                psteps[0] += 1
                ins.then_inc(pool_step, 1)
                pool.wait_ge(pool_step, psteps[0])

            nc.gpsimd.memset(minus_half, -0.5)
            nc.gpsimd.memset(ones_f[:, :], 1.0)
            nc.gpsimd.memset(tiny, 0.0)
            nc.gpsimd.iota(iota_t[:, :], [[1, T]], base=0, channel_multiplier=0, allow_small_or_imprecise_dtypes=True)
            nc.gpsimd.memset(half_pi, float(np.float32(np.pi / 2))).then_inc(pool_init, 1)
            pool.wait_ge(pool_init, 1)

            def s5_uk(i):
                if i >= 1:
                    pool.wait_ge(s5_frac, i)
                nc.gpsimd.tensor_scalar(s5u, iota_t[:, :], phi_hi[:, i:i + 1], None, ALU.mult)
                nc.gpsimd.tensor_scalar(s5k, iota_t[:, :], phi[:, i:i + 1], MAGIC, ALU.mult, ALU.add).then_inc(s5_uk_sem, 1)

            def s5_rotate(i):
                pool.wait_ge(s5_z, i + 1)
                if i >= 1:
                    pool.wait_ge(s5_x, i)
                if i >= 2:
                    j = i - 2
                    if j % 4 == 3:
                        pool.wait_ge(psum_full, plan.full("s5y", j // 4))
                    else:
                        pool.wait_ge(s5_used, j + 1 - (j + 1) // 4)
                c, s = s5cos[i % 2], s5sin[i % 2]
                zr, zi, xr, xi = s5zr[i % 2], s5zi[i % 2], s5xr[i % 2], s5xi[i % 2]
                op = nc.gpsimd.tensor_tensor
                op(xr, zr, c, ALU.mult)
                link(op(s5xt, zi, s, ALU.mult))
                link(op(xr, xr, s5xt, ALU.subtract))
                op(xi, zr, s, ALU.mult)
                link(op(s5xt, zi, c, ALU.mult))
                op(xi, xi, s5xt, ALU.add).then_inc(s5_x, 1)

            pool.wait_ge(s5_phi, 1)
            s5_uk(0)
            s5_uk(1)
            for i in range(NST):
                if i == 2:
                    answer()
                if i + 2 < NST:
                    s5_uk(i + 2)
                s5_rotate(i)
                if i == 3:
                    pool.wait_ge(s5_x, 4)
                    pool.wait_ge(krope_ready, 1)
                    for h in range(H1):
                        nc.gpsimd.tensor_copy(fm(khat, h)[64:128, :], krope[64:128, :]).then_inc(khat_ready, 1)
                    pool.wait_ge(khat_ready, H1)
            answer(2)
            answer(4)
            answer(4)
            link(nc.gpsimd.memset(zero_i, 0))
            pool.dma_start(scratch["tab"].rearrange("(p c) o -> p (c o)", p=P), zero_i).then_inc(tab_zero, 16)
            pool.wait_ge(tab_zero, 16)
            pool.wait_ge(route_addr, 1)
            for j in range(32):
                pool.indirect_dma_start(scratch["tab"], bass.IndirectOffsetOnAxis(ap=addr_i[:, j:j + 1].bitcast(U32), axis=0),
                                        tok_i[:, j // 8:j // 8 + 1], None).then_inc(ids_sent, 16)
            pool.wait_ge(ids_sent, 16 * 32)
            pool.dma_start(slot_tok, scratch["tab"].rearrange("(p c) o -> p (c o)", p=P)).then_inc(ids_back, 16)
            pool.wait_ge(ids_back, 16)
            pool.wait_ge(x2_stored, 16 * NT)

            def gather(u, b, first=False):
                e = 2 * u + b
                if not first:
                    pool.wait_ge(gathered[b], 16 * u)
                    pool.wait_ge(xtr_full, e - 1)
                nc.gpsimd.tensor_copy(idx_cur[:, b:b + 1], slot_tok[:, bass.ds(e, 1)]).then_inc(idx_ready, 1)
                pool.wait_ge(idx_ready, e + 1)
                nc.gpsimd.tensor_tensor(spare, minus_half[:, 0:1], minus_half[:, 0:1], ALU.mult)
                pool.indirect_dma_start(xg[b], None, scratch["x2"], bass.IndirectOffsetOnAxis(ap=idx_cur[:, b:b + 1].bitcast(U32), axis=0)
                                        ).then_inc(gathered[b], 16)

            gather(0, 0, True)
            gather(0, 1, True)
            with pool.Fori(1, NE // 2) as u:
                gather(u, 0)
                gather(u, 1)
            pool.wait_ge(route_ctrl, 2)
            pool.wait_ge(xtr_full, NE)
            for b in range(2):
                pool.wait_ge(y_stored[b], 16 * NE // 2)
            n_ov = pool.value_load(ctrl_i[0:1, 31:32], min_val=0, max_val=NOV)
            with pool.Fori(0, NOV) as o:
                with pool.If(n_ov > o):
                    nc.gpsimd.tensor_copy(idx_cur[:, 0:1], slot_tok[:, bass.ds(o + NE, 1)]).then_inc(ov["idx"], 1)
                    pool.wait_ge(ov["idx"], o + 1)
                    nc.gpsimd.tensor_tensor(spare, minus_half[:, 0:1], minus_half[:, 0:1], ALU.mult)
                    pool.indirect_dma_start(xg[0], None, scratch["x2"], bass.IndirectOffsetOnAxis(ap=idx_cur[:, 0:1].bitcast(U32), axis=0)
                                            ).then_inc(ov["gather"], 16)
                    pool.wait_ge(ov["store"], 16 * o + 16)

            def gather_outputs(rows):
                for j in range(32):
                    if j >= 4:
                        pool.wait_ge(combined, j - 3)
                    pool.indirect_dma_start(ygath[j % 4], None, rows,
                                            bass.IndirectOffsetOnAxis(ap=yrow_i[:, j:j + 1].bitcast(U32), axis=0)
                                            ).then_inc(ygot[j % 4], 16)

            with pool.If(n_ov > 0):
                pool.wait_ge(y_zeroed, 16)
                gather_outputs(scratch["y"])
            with pool.If(n_ov < 1):
                gather_outputs(scratch["y"][0:NE * P, :])
            answer(len(REQUESTS) - answered[0])
            assert answered[0] == len(REQUESTS)


def kernel(**inputs):
    import concourse.bacc as bacc
    from concourse.bass_utils import run_bass_kernel_spmd

    w = {k: np.asarray(x) for k, x in inputs.items()}
    x = w["x"][0]
    consts = host_consts()
    rows = np.zeros((len(ROWS), D), np.float32)
    for i, n in enumerate(("ln1_g", "ln1_b", "ln2_g", "ln2_b", "ln3_g", "ln3_b")):
        rows[i] = w[n][0]
    rows[6] = w["final_norm_w_2"]
    rows[7, :512] = w["gmlp_norm_w_2"][0]
    rows[8, :24] = w["gate_b_2"][0]
    rows[9, :64] = w["router_bias"][0]
    w2 = np.stack([w["cmp_k_w2_2"][0], w["cmp_v_w2_2"][0]]).reshape(2, 2, P, 64)
    arrays = {
        "x_fm": x.T.reshape(KD, P, T).transpose(1, 0, 2).reshape(P, KD * T),
        "x_tm": x.reshape(NT, P, D).transpose(1, 0, 2).reshape(P, NT * D),
        "mem": w["mem"][0],
        "positions": w["positions"].reshape(1, T),
        "stream": host_stream(w),
        "cols": host_cols(w),
        "const": np.concatenate([consts[k] for k in CONST_AT if k != "width"], 1),
        "rows": rows,
        "zeros": np.zeros((1, D), np.float32),
        "s5": host_s5(w),
        "w_router": w["w_router"][0].reshape(KD, P, NE).transpose(1, 0, 2).reshape(P, KD * NE),
        "cmp_w2": w2.transpose(2, 0, 1, 3).reshape(P, 256),
        "gmlp_ws": w["gmlp_ws_2"][0].transpose(2, 0, 1),
        "w_exp_gu": w["w_exp_gu"][0],
        "w_exp_down": w["w_exp_down"][0],
    }
    arrays = {k: np.ascontiguousarray(v) for k, v in arrays.items()}
    nc = bacc.Bacc("TRN2", target_bir_lowering=False, num_devices=1)
    a = {k: nc.dram_tensor(k, v.shape, mybir.dt.from_np(v.dtype), kind="ExternalInput").ap() for k, v in arrays.items()}
    out = nc.dram_tensor("out", (T, D), F32, kind="ExternalOutput").ap()
    scratch = {
        "x2": nc.dram_tensor("x2_rows", (T, D), F32).ap(),
        "y": nc.dram_tensor("y_rows", (NBLK * P, D), F32).ap(),
        "tab": nc.dram_tensor("slot_table", (P * TABW, 1), I32).ap(),
    }
    build(nc, a, out, scratch)
    r = run_bass_kernel_spmd(nc, [arrays], core_ids=[0])
    return np.asarray(r.results[0]["out"]).reshape(1, T, D)
```
